# Optimizing a Trainium2 kernel written in Bass

```python
import jax, jax.numpy as jnp
from jax import lax
import numpy as np

D_MODEL = 1024
BATCH = 1
SEQ = 128
DEPTH = 2
DEC_BATCH = 1
DEC_SEQ = 512
PAST_LEN = 128

GRID_W = 64
N_MIXERS = 2
N_ATTN_LAYERS = (DEPTH + N_MIXERS - 1) // N_MIXERS
N_POOL_LAYERS = DEPTH // N_MIXERS
N_HEADS = 8
N_KV_HEADS = 2
HEAD_DIM = 128
GROUP = N_HEADS // N_KV_HEADS
QKV_DIM = (N_HEADS + 2 * N_KV_HEADS) * HEAD_DIM
ROPE_AXIS_DIM = HEAD_DIM // 2
ROPE_THETA = 10000.0
Q_BLOCK = 128
POOL_WINDOWS = (2, 4, 8, 16)
N_POOL_GROUPS = 4
POOL_GROUP_DIM = D_MODEL // N_POOL_GROUPS
PEER_HEADS = 8
PEER_N_KEYS = 128
PEER_N_EXPERTS = PEER_N_KEYS * PEER_N_KEYS
PEER_TOPK = 16
PEER_QUERY_DIM = 256
PEER_HALF = PEER_QUERY_DIM // 2
PEER_BLOCK = 128
EPS = 1e-6

kernel_name = "hybrid_dit_gqa_pool_peer_step"

def rmsnorm(x, g):
    xf = x.astype(jnp.float32)
    y = xf * lax.rsqrt(jnp.mean(xf * xf, axis=-1, keepdims=True) + EPS)
    return y.astype(x.dtype) * g

def adaln(cond, w, b):
    m = jax.nn.silu(cond) @ w + b
    return jnp.split(m, 6, axis=-1)

def modulate(x, g, shift, scale):
    return rmsnorm(x, g) * (1.0 + scale) + shift

def grid_rope_tables(n):
    rows = n // GRID_W
    row = jnp.repeat(jnp.arange(rows), GRID_W).astype(jnp.float32)
    col = jnp.tile(jnp.arange(GRID_W), rows).astype(jnp.float32)
    half = ROPE_AXIS_DIM // 2
    inv = jnp.power(ROPE_THETA, -jnp.arange(half, dtype=jnp.float32) / half)
    ar = row[:, None] * inv[None, :]
    ac = col[:, None] * inv[None, :]
    return (jnp.cos(ar), jnp.sin(ar), jnp.cos(ac), jnp.sin(ac))

def rotate(x, cos, sin):
    half = x.shape[-1] // 2
    cos = cos[:, None, :].astype(x.dtype)
    sin = sin[:, None, :].astype(x.dtype)
    x1, x2 = x[..., :half], x[..., half:]
    return jnp.concatenate([x1 * cos - x2 * sin, x1 * sin + x2 * cos], axis=-1)

def apply_rope2d(x, tables):
    cr, sr, cc, sc = tables
    return jnp.concatenate([rotate(x[..., :ROPE_AXIS_DIM], cr, sr),
                            rotate(x[..., ROPE_AXIS_DIM:], cc, sc)], axis=-1)

def qkv_proj(h, w_qkv, q_g, k_g):
    b, s, _ = h.shape
    qkv = h @ w_qkv
    nq = N_HEADS * HEAD_DIM
    nk = N_KV_HEADS * HEAD_DIM
    q = qkv[..., :nq].reshape(b, s, N_HEADS, HEAD_DIM)
    k = qkv[..., nq:nq + nk].reshape(b, s, N_KV_HEADS, HEAD_DIM)
    v = qkv[..., nq + nk:].reshape(b, s, N_KV_HEADS, HEAD_DIM)
    return rmsnorm(q, q_g), rmsnorm(k, k_g), v

def block_attention(q, k, v):
    b, s = q.shape[:2]
    nb = s // Q_BLOCK
    qb = q.reshape(b, nb, Q_BLOCK, N_KV_HEADS, GROUP, HEAD_DIM).transpose(1, 0, 2, 3, 4, 5)
    scale = HEAD_DIM ** -0.5

    def one(qi):
        sc = jnp.einsum('bqkgd,btkd->bkgqt', qi, k).astype(jnp.float32) * scale
        p = jax.nn.softmax(sc, axis=-1).astype(v.dtype)
        return jnp.einsum('bkgqt,btkd->bqkgd', p, v)

    o = lax.map(one, qb)
    return o.transpose(1, 0, 2, 3, 4, 5).reshape(b, s, N_HEADS * HEAD_DIM)

def pool_mixer(h, w, scale):
    b, s, _ = h.shape
    hf = h.astype(jnp.float32)
    t = jnp.arange(s)
    outs = []
    for j, win in enumerate(POOL_WINDOWS):
        xg = hf[..., j * POOL_GROUP_DIM:(j + 1) * POOL_GROUP_DIM]
        cs = jnp.concatenate([jnp.zeros((b, 1, POOL_GROUP_DIM), jnp.float32), jnp.cumsum(xg, axis=1)], axis=1)
        lo = jnp.clip(t - win // 2, 0, s)
        hi = jnp.clip(t + win // 2, 0, s)
        mean = (cs[:, hi] - cs[:, lo]) / (hi - lo).astype(jnp.float32)[None, :, None]
        outs.append((mean - xg).astype(h.dtype) @ w[j])
    return jnp.concatenate(outs, axis=-1) * scale

def peer(h, wq, keys, u, v):
    b, s, d = h.shape
    x = h.reshape(-1, d)
    t = x.shape[0]
    q = (x @ wq).reshape(t, PEER_HEADS, 2, PEER_HALF)
    sc = jnp.einsum('thpc,hpnc->thpn', q, keys).astype(jnp.float32)
    s_top, i_top = lax.top_k(sc, PEER_TOPK)
    cand = (s_top[:, :, 0, :, None] + s_top[:, :, 1, None, :]).reshape(t, PEER_HEADS, PEER_TOPK * PEER_TOPK)
    cs, ci = lax.top_k(cand, PEER_TOPK)
    i1 = jnp.take_along_axis(i_top[:, :, 0], ci // PEER_TOPK, axis=-1)
    i2 = jnp.take_along_axis(i_top[:, :, 1], ci % PEER_TOPK, axis=-1)
    idx = i1 * PEER_N_KEYS + i2
    g = jax.nn.softmax(cs, axis=-1).astype(h.dtype)
    nb = t // PEER_BLOCK
    xb = x.reshape(nb, PEER_BLOCK, d)
    ib = idx.reshape(nb, PEER_BLOCK, PEER_HEADS, PEER_TOPK)
    gb = g.reshape(nb, PEER_BLOCK, PEER_HEADS, PEER_TOPK)

    def one(args):
        xi, ii, gi = args
        a = jnp.einsum('thkd,td->thk', u[ii], xi)
        act = jax.nn.gelu(a, approximate=False) * gi
        return jnp.einsum('thk,thkd->td', act, v[ii])

    out = lax.map(one, (xb, ib, gb))
    return out.reshape(b, s, d)

def setup_inputs(seed: int = 0) -> dict:
    key = jax.random.key(seed)
    ks = jax.random.split(key, 24)
    f32 = jnp.float32
    nrm = lambda k, shp: jax.random.normal(k, shp, f32)
    return {
        "x_prompt": nrm(ks[0], (BATCH, SEQ, D_MODEL)),
        "x_sample": nrm(ks[1], (DEC_BATCH, DEC_SEQ, D_MODEL)),
        "cache_k": nrm(ks[2], (DEC_BATCH, N_ATTN_LAYERS, PAST_LEN, N_KV_HEADS, HEAD_DIM)),
        "cache_v": nrm(ks[3], (DEC_BATCH, N_ATTN_LAYERS, PAST_LEN, N_KV_HEADS, HEAD_DIM)),
        "c": nrm(ks[4], (DEC_BATCH, D_MODEL)),
        "c_ctx": nrm(ks[5], (D_MODEL,)),
        "ada_w": nrm(ks[6], (DEPTH, D_MODEL, 6 * D_MODEL)) * (0.5 * D_MODEL ** -0.5),
        "ada_b": nrm(ks[7], (DEPTH, 6 * D_MODEL)) * 0.02,
        "norm_mix_g": 1.0 + 0.1 * nrm(ks[8], (DEPTH, D_MODEL)),
        "norm_ffn_g": 1.0 + 0.1 * nrm(ks[9], (DEPTH, D_MODEL)),
        "final_norm_g": 1.0 + 0.1 * nrm(ks[10], (D_MODEL,)),
        "attn_w_qkv": nrm(ks[11], (N_ATTN_LAYERS, D_MODEL, QKV_DIM)) * D_MODEL ** -0.5,
        "attn_q_norm_g": 1.0 + 0.1 * nrm(ks[12], (N_ATTN_LAYERS, HEAD_DIM)),
        "attn_k_norm_g": 1.0 + 0.1 * nrm(ks[13], (N_ATTN_LAYERS, HEAD_DIM)),
        "attn_w_o": nrm(ks[14], (N_ATTN_LAYERS, N_HEADS * HEAD_DIM, D_MODEL)) * (N_HEADS * HEAD_DIM) ** -0.5,
        "pool_w": nrm(ks[15], (N_POOL_LAYERS, N_POOL_GROUPS, POOL_GROUP_DIM, POOL_GROUP_DIM)) * POOL_GROUP_DIM ** -0.5,
        "pool_scale": 1.0 + 0.1 * nrm(ks[16], (N_POOL_LAYERS, D_MODEL)),
        "peer_wq": nrm(ks[17], (DEPTH, D_MODEL, PEER_HEADS * PEER_QUERY_DIM)) * D_MODEL ** -0.5,
        "peer_keys": nrm(ks[18], (DEPTH, PEER_HEADS, 2, PEER_N_KEYS, PEER_HALF)) * PEER_HALF ** -0.5,
        "peer_u": nrm(ks[19], (DEPTH, PEER_N_EXPERTS, D_MODEL)) * D_MODEL ** -0.5,
        "peer_v": nrm(ks[20], (DEPTH, PEER_N_EXPERTS, D_MODEL)),
    }

def reference(x_prompt, x_sample, cache_k, cache_v, c, c_ctx, ada_w, ada_b, norm_mix_g, norm_ffn_g,
              final_norm_g, attn_w_qkv, attn_q_norm_g, attn_k_norm_g, attn_w_o, pool_w, pool_scale,
              peer_wq, peer_keys, peer_u, peer_v):
    x = x_prompt
    new_k_list = []
    new_v_list = []
    for i in range(DEPTH):
        sh1, sc1, g1, sh2, sc2, g2 = adaln(c_ctx, ada_w[i], ada_b[i])
        h = modulate(x, norm_mix_g[i], sh1, sc1)
        j = i // N_MIXERS
        if i % N_MIXERS == 0:
            q, k, v = qkv_proj(h, attn_w_qkv[j], attn_q_norm_g[j], attn_k_norm_g[j])
            new_k_list.append(k)
            new_v_list.append(v)
            mix = block_attention(q, k, v) @ attn_w_o[j]
        else:
            mix = pool_mixer(h, pool_w[j], pool_scale[j])
        x = x + g1 * mix
        h = modulate(x, norm_ffn_g[i], sh2, sc2)
        x = x + g2 * peer(h, peer_wq[i], peer_keys[i], peer_u[i], peer_v[i])
    y_prompt = rmsnorm(x, final_norm_g)
    new_k = jnp.stack(new_k_list, axis=1)
    new_v = jnp.stack(new_v_list, axis=1)

    x = x_sample
    tables = grid_rope_tables(x_sample.shape[1])
    for i in range(DEPTH):
        sh1, sc1, g1, sh2, sc2, g2 = [m[:, None, :] for m in adaln(c, ada_w[i], ada_b[i])]
        h = modulate(x, norm_mix_g[i], sh1, sc1)
        j = i // N_MIXERS
        if i % N_MIXERS == 0:
            q, k, v = qkv_proj(h, attn_w_qkv[j], attn_q_norm_g[j], attn_k_norm_g[j])
            q = apply_rope2d(q, tables)
            k = apply_rope2d(k, tables)
            k_all = jnp.concatenate([cache_k[:, j], k], axis=1)
            v_all = jnp.concatenate([cache_v[:, j], v], axis=1)
            mix = block_attention(q, k_all, v_all) @ attn_w_o[j]
        else:
            mix = pool_mixer(h, pool_w[j], pool_scale[j])
        x = x + g1 * mix
        h = modulate(x, norm_ffn_g[i], sh2, sc2)
        x = x + g2 * peer(h, peer_wq[i], peer_keys[i], peer_u[i], peer_v[i])
    y_sample = rmsnorm(x, final_norm_g)

    return (y_prompt, y_sample, new_k, new_v)


_drawn_inputs = setup_inputs


def setup_inputs(seed=0):
    import zlib

    import numpy as np

    out = dict(_drawn_inputs(seed))
    spreads = {}
    factors = {'attn_q_norm_g': 2.679}
    for name, (base, spread) in spreads.items():
        noise = np.random.default_rng([zlib.crc32(name.encode()), seed]).standard_normal(out[name].shape)
        drawn = base * np.exp(spread * noise) if base else spread * noise
        out[name] = __import__('jax').numpy.asarray(drawn.astype(out[name].dtype))
    for name, factor in factors.items():
        out[name] = (out[name] * factor).astype(out[name].dtype)
    return out
```

```python
from contextlib import ExitStack

import numpy as np
import concourse.bass as bass
from concourse import mybir

ALU = mybir.AluOpType
ACT = mybir.ActivationFunctionType
AX = mybir.AxisListType
F32 = mybir.dt.float32
U32 = mybir.dt.uint32

P = 128
D = 1024
K = D // P
DEPTH = 2
TS, TP = 512, 128
T = TS + TP
TILES = T // P
SEGS = ((0, TS), (TS, T))
NH, NKV, HD = 8, 2, 128
KT = (P + TS) // P
SCALE = HD ** -0.5
EPS = 1e-6
WINDOWS = (2, 4, 8, 16)
PH, NKEY, TOPK = 8, 128, 16
HP = 2 * PH
NE = NKEY * NKEY
CH = 512
PAD = 8
PW = PAD + TS + 2 * PAD + TP + PAD
PSEG = ((PAD, PAD + TS), (3 * PAD + TS, 3 * PAD + T))
LOWEST = -3.0e38
RING, GRP = 8, 4
ITERS = P // RING

O_C = 0
O_B = O_C + 2 * K
O_G = O_B + DEPTH * 6 * K
O_H = O_G + 5 * K
O_PS = O_H + 2
N_SMALL = O_PS + K
C_ID, C_ONE, C_ROT, C_IO = 0, P, 2 * P, 3 * P
N_CONST = 4 * P


def order_of_units():
    o = [(("ada", 0, j), "A") for j in range(12)]
    o += [(("norm", 0), "A")]
    for s in range(NH + NKV + 2):
        if s < NH + NKV:
            o.append((("proj", s), "A"))
        if 1 <= s < NH + NKV + 1:
            o.append((("hsum", s - 1), "A"))
        if s >= 2:
            o.append((("rot", s - 2), "D"))
    o += [(("v", t), "A") for t in range(TILES)]
    n_att = NH * TILES
    for n in range(n_att + 2):
        if n < n_att:
            o.append((("score", n), "A"))
        if 1 <= n <= n_att:
            o.append((("pt", n - 1), "D"))
        if n >= 2 and (n - 2) % TILES == TILES - 1:
            o.append((("pv", (n - 2) // TILES), "A"))
    o += [(("wo", m), "D") for m in range(K)]
    for L in range(DEPTH):
        if L:
            o += [(("norm", 2), "A")]
            o += [(("pool", m), "D") for m in range(K)]
        o += [(("norm", 2 * L + 1), "A")]
        o += [(("wq", L, c), "A") for c in range(HP)]
        o += [(("sc", L, t, half), "A") for t in range(TILES) for half in range(2)]
        for t in range(TILES):
            o.append((("htok", L, t), "A"))
            if t == 0 and L == 0:
                o += [(("ada", 1, j), "A") for j in range(12)]
            o.append((("ob", L, t), "D"))
    o += [(("norm", 4), "A")]
    return o


def build(nc, ins, outs):
    xT_d, small_d, const_d, trig_d, inv_d, ck_d, cv_d, ada_d, qkv_d, wo_d, pw_d, wq_d, keys_d, u_d, v_d = ins
    y_d, nk_d, nv_d = outs

    ORDER = order_of_units()
    A, Dn = {}, {}
    for name, cls in ORDER:
        table = A if cls == "A" else Dn
        table[name] = len(table)

    chunks = [(("ada", 0, j), ("ada", 0, j)) for j in range(12)]
    chunks += [(("qkv", 0), ("proj", 3)), (("qkv", 1), ("proj", 7)), (("qkv", 2), ("v", TILES - 1))]
    chunks += [(("wo", 0), ("wo", 3)), (("wo", 1), ("wo", 7))]
    chunks += [(("wq", 0, i), ("wq", 0, 4 * i + 3)) for i in range(4)]
    chunks += [(("ada", 1, j), ("ada", 1, j)) for j in range(12)]
    chunks += [(("pool",), ("pool", K - 1))]
    chunks += [(("wq", 1, i), ("wq", 1, 4 * i + 3)) for i in range(4)]
    CN = {c[0]: n for n, c in enumerate(chunks)}

    with ExitStack() as ctx:
        def sb(name, shape, dt=F32, where=None):
            return (where or ctx).enter_context(nc.sbuf_tensor(name, shape, dt))

        def sem(name):
            return ctx.enter_context(nc.semaphore(name))

        bankA = [ctx.enter_context(nc.psum_tensor(f"bankA{i}", [P, 1024], F32)) for i in range(2)]
        bankD = [ctx.enter_context(nc.psum_tensor(f"bankD{i}", [P, 1024], F32)) for i in range(2)]

        xT = sb("xT", [P, K, T])
        hT = sb("hT", [P, K, T])
        sq = sb("sq", [P, K, T])
        std = sb("std", [P, T])
        wch = sb("wch", [P, 2, K * CH])
        qT = sb("qT", [P, HP, T])
        keys = sb("keys", [P, HP, NKEY])
        small = sb("small", [P, N_SMALL])
        const = sb("const", [P, N_CONST])
        epsb = sb("epsb", [P, 1])
        cs = sb("cs", [P, K, 2])
        mod = sb("mod", [P, DEPTH, 6, K, 2])
        amod = sb("amod", [P, DEPTH, 2, K, 2])
        idx = sb("idx", [P, TILES * P], U32)
        gate = sb("gate", [P, TILES * P])
        aval = sb("aval", [P, P])
        actg = sb("actg", [P, P])
        a8 = sb("a8", [P, RING])
        gsum = sb("gsum", [P, TILES * PH])
        idxc = sb("idxc", [P, 2, GRP], U32)

        QT, OT = qT[:, 0:NH, :], qT[:, NH:2 * NH, :]
        PT = sq[:, :, :].rearrange("p k t -> p (k t)").rearrange("p (b j q) -> p b j q", b=2, j=KT)
        ident = const[:, C_ID:C_ID + P]
        ones = const[:, C_ONE:C_ONE + P]
        rotp = const[:, C_ROT:C_ROT + P]
        iota = const[:, C_IO:C_IO + P]

        with ExitStack() as att:
            trig = sb("trig", [P, 2, TS], where=att)
            kA = sb("kA", [P, NKV, KT * P], where=att)
            kP = sb("kP", [P, NKV, P], where=att)
            vA = sb("vA", [P, KT, NKV * HD], where=att)
            vP = sb("vP", [P, NKV * HD], where=att)
            PTp = sb("PTp", [P, 2, P], where=att)
            prob = sb("prob", [P, 2, KT * P], where=att)
            qraw = sb("qraw", [P, 2, T], where=att)
            hsq = sb("hsq", [P, 2, T], where=att)
            hstd = sb("hstd", [P, 2, T], where=att)
            qn = sb("qn", [P, 2, TS], where=att)
            ropes = sb("ropes", [P, 2, TS], where=att)
            smx = sb("smx", [P, 2, 4], where=att)
        with ExitStack() as rt:
            sc = sb("sc", [P, HP, NKEY], where=rt)
            sc2 = sb("sc2", [P, HP, NKEY], where=rt)
            mask = sb("mask", [P, PH * TOPK, TOPK], where=rt)
            top = sb("top", [P, HP, TOPK], where=rt)
            topi = sb("topi", [P, HP, TOPK], U32, where=rt)
            topf = sb("topf", [P, HP, TOPK], where=rt)
            csv = sb("csv", [P, PH, TOPK], where=rt)
            csi = sb("csi", [P, PH, TOPK], U32, where=rt)
            pick = sb("pick", [P, 2, PH * TOPK], U32, where=rt)
            pickf = sb("pickf", [P, 2, PH * TOPK], where=rt)
            i12 = sb("i12", [P, 2, PH * TOPK], where=rt)
        with ExitStack() as gs:
            rows = sb("rows", [P, RING, D], where=gs)
            htok = sb("htok", [P, D], where=gs)
            acc = sb("acc", [P, 2, D], where=gs)
        with ExitStack() as pl:
            inv = sb("inv", [P, 4, T], where=pl)
            pad = sb("pad", [P, 3, 2, PW], where=pl)

        small_ready = sem("small_ready")
        in_ready = sem("in_ready")
        att_in = sem("att_in")
        keys_ready = sem("keys_ready")
        inv_ready = sem("inv_ready")
        chunk_ready = [sem(f"chunk_ready{i}") for i in range(2)]
        row_ready = [sem(f"row_ready{i}") for i in range(RING)]
        a_full = sem("a_full")
        a_free = sem("a_free")
        d_full = sem("d_full")
        d_free = sem("d_free")
        cond_ready = sem("cond_ready")
        sq_ready = sem("sq_ready")
        h_ready = sem("h_ready")
        hsq_ready = sem("hsq_ready")
        qn_ready = sem("qn_ready")
        rope_done = sem("rope_done")
        negmax_ready = sem("negmax_ready")
        prob_ready = sem("prob_ready")
        pooled_ready = sem("pooled_ready")
        sc_used = sem("sc_used")
        gexp_in = sem("gexp_in")
        gexp_out = sem("gexp_out")
        idx_ready = sem("idx_ready")
        idx_copied = sem("idx_copied")
        rows_free = sem("rows_free")
        u_done = sem("u_done")
        gelu_done = sem("gelu_done")
        acc_ready = sem("acc_ready")
        step = sem("step")
        y_ready = sem("y_ready")
        dve_passed = sem("dve_passed")
        pool_passed = sem("pool_passed")
        out_done = sem("out_done")

        block = ctx.enter_context(nc.Block())

        @block.sync
        def _(sp):
            def source(name):
                if name[0] == "ada":
                    return ada_d[name[1], name[2]]
                if name[0] == "qkv":
                    return qkv_d[name[1]]
                if name[0] == "wo":
                    return wo_d[name[1]]
                if name[0] == "wq":
                    return wq_d[name[1], name[2]]
                return pw_d

            sp.dma_start(small[:, :], small_d).then_inc(small_ready, 16)
            for n, (name, last) in enumerate(chunks):
                if n >= 2:
                    u = chunks[n - 2][1]
                    if u in A:
                        sp.wait_ge(a_full, A[u] + 1)
                    else:
                        sp.wait_ge(d_full, Dn[u] + 1)
                src = source(name)
                sp.dma_start(wch[:, n % 2, 0:src.shape[1]], src).then_inc(chunk_ready[n % 2], 16)
                if n == 1:
                    sp.dma_start(const[:, :], const_d).then_inc(in_ready, 16)
                    sp.dma_start(xT[:, :, :], xT_d).then_inc(in_ready, 16)
                    sp.dma_start(trig[:, :, :], trig_d).then_inc(att_in, 16)
                    sp.dma_start(kA[:, :, 0:P], ck_d).then_inc(att_in, 16)
                    sp.dma_start(vA[:, 0, :], cv_d).then_inc(att_in, 16)
                    sp.dma_start(keys[:, :, :], keys_d[0]).then_inc(keys_ready, 16)
                if name == ("wo", 1):
                    sp.wait_ge(rope_done, NH + NKV)
                    sp.dma_start(nk_d, kP[:, :, :]).then_inc(out_done, 16)
                    sp.wait_ge(a_free, A[("v", TILES - 1)] + 1)
                    sp.dma_start(nv_d, vP[:, :]).then_inc(out_done, 16)
                if name == ("ada", 1, 11):
                    sp.wait_ge(a_full, A[("sc", 0, TILES - 1, 1)] + 1)
                    sp.dma_start(keys[:, :, :], keys_d[1]).then_inc(keys_ready, 16)
                if name == ("pool",):
                    sp.wait_ge(d_full, Dn[("ob", 0, TILES - 1)] + 1)
                    sp.dma_start(inv[:, :, :], inv_d).then_inc(inv_ready, 16)
            sp.wait_ge(y_ready, 1)
            sp.dma_start(y_d, hT[:, :, :]).then_inc(out_done, 16)
            sp.wait_ge(out_done, 48)

        @block.gpsimd
        def _(pool):
            for L in range(DEPTH):
                pool.wait_ge(idx_ready, L + 1)
                with pool.Fori(0, TILES) as t:
                    for stage, table in enumerate((u_d.rearrange("l e d -> (l e) d"), v_d.rearrange("l e d -> (l e) d"))):
                        with pool.Fori(0, ITERS) as i:
                            it = ((t + L * TILES) * 2 + stage) * ITERS + i
                            for g in range(2):
                                pool.wait_ge(rows_free, it * RING + (g * GRP + GRP))
                                pool.tensor_copy(idxc[:, g, :], idx[:, bass.ds(t * P + i * RING + g * GRP, GRP)]
                                                 ).then_inc(idx_copied, 1)
                                pool.wait_ge(idx_copied, it * 2 + (g + 1))
                                pool.sem_inc(pool_passed, 1)
                                for j in range(GRP):
                                    s = g * GRP + j
                                    pool.indirect_dma_start(
                                        out=rows[:, s, :], out_offset=None, in_=table,
                                        in_offset=bass.IndirectOffsetOnAxis(ap=idxc[:, g, j:j + 1], axis=0),
                                    ).then_inc(row_ready[s], 16)

        @block.scalar
        def _(act):
            act.wait_ge(small_ready, 16)
            act.activation(cs[:, :, :].rearrange("p k c -> p (k c)"), small[:, O_C:O_C + 2 * K],
                           ACT.Silu).then_inc(cond_ready, 1)
            for name, cls in ORDER:
                if cls != "A":
                    continue
                n = A[name]
                bank = bankA[n % 2]
                kind = name[0]
                if kind == "norm":
                    i = name[1]
                    if i == 0:
                        act.wait_ge(in_ready, 32)
                        act.wait_ge(step, 1)
                    else:
                        before = {1: ("wo", K - 1), 2: ("ob", 0, TILES - 1), 3: ("pool", K - 1),
                                  4: ("ob", 1, TILES - 1)}[i]
                        act.wait_ge(d_free, Dn[before] + 1)
                    act.activation(sq[:, :, :], xT[:, :, :], ACT.Square).then_inc(sq_ready, 1)
                    act.wait_ge(a_full, n + 1)
                    act.activation(std[:, :], bank[:, 0:T], ACT.Sqrt, bias=epsb[:, 0:1],
                                   scale=1.0 / D).then_inc(a_free, 1)
                    continue
                if kind in ("proj", "hsum") and name[1] >= 2:
                    act.wait_ge(qn_ready, name[1] - 1)
                if kind == "score":
                    act.wait_ge(negmax_ready, name[1] + 1)
                    if name[1] >= 2:
                        act.wait_ge(d_full, Dn[("pt", name[1] - 2)] + 1)
                if kind == "sc" and name[3] == 0 and name[1] * TILES + name[2] > 0:
                    act.wait_ge(sc_used, name[1] * TILES + name[2])
                if kind == "sc" and name[2] == 0 and name[3] == 0:
                    pass
                if kind == "htok" and name[2] > 0:
                    act.wait_ge(u_done, name[1] * TILES + name[2])
                act.wait_ge(a_full, n + 1)
                if kind == "ada":
                    L, j = name[1:]
                    act.copy(mod[:, L, j // 2, 4 * (j % 2):4 * (j % 2) + 4, :],
                             bank[:, 0:8].rearrange("p (m c) -> p m c", c=2)).then_inc(a_free, 1)
                elif kind == "proj":
                    b = name[1] % 2
                    act.activation(hsq[:, b, :], bank[:, 0:T], ACT.Square).then_inc(hsq_ready, 1)
                    act.copy(qraw[:, b, :], bank[:, 0:T]).then_inc(a_free, 1)
                elif kind == "hsum":
                    act.activation(hstd[:, name[1] % 2, :], bank[:, 0:T], ACT.Sqrt, bias=epsb[:, 0:1],
                                   scale=1.0 / HD).then_inc(a_free, 1)
                elif kind == "v":
                    dst = vA[:, 1 + name[1], :] if name[1] < TILES - 1 else vP[:, :]
                    act.copy(dst, bank[:, 0:NKV * HD]).then_inc(a_free, 1)
                elif kind == "score":
                    b = name[1] % 2
                    w = KT * P if name[1] % TILES < TILES - 1 else P
                    act.activation(prob[:, b, 0:w], bank[:, 0:w], ACT.Exp, bias=smx[:, b, 1:2],
                                   scale=SCALE, accum_out=smx[:, b, 2:3]).then_inc(a_free, 1)
                elif kind == "pv":
                    act.copy(OT[:, name[1], :], bank[:, 0:T]).then_inc(a_free, 1)
                elif kind == "wq":
                    act.copy(qT[:, name[2], :], bank[:, 0:T]).then_inc(a_free, 1)
                elif kind == "sc":
                    h0 = name[3] * PH
                    act.copy(sc[:, h0:h0 + PH, :], bank[:, :].rearrange("p (h n) -> p h n", n=NKEY)
                             ).then_inc(a_free, 1)
                    if name[2] == TILES - 1 and name[3] == 1:
                        act.wait_ge(gexp_in, name[1] + 1)
                        act.activation(gate[:, :], gate[:, :], ACT.Exp).then_inc(gexp_out, 1)
                elif kind == "htok":
                    act.copy(htok[:, :], bank[:, :]).then_inc(a_free, 1)
                if kind == "htok" and not (name[1] == 0 and name[2] == 0) or name == ("ada", 1, 11):
                    L, t = name[1:] if kind == "htok" else (0, 0)
                    act.wait_ge(u_done, L * TILES + t + 1)
                    act.activation(actg[:, :], aval[:, :], ACT.Gelu).then_inc(gelu_done, 1)

        @block.vector
        def _(v):
            steps = [0]

            def then(ins):
                steps[0] += 1
                ins.then_inc(step, 1)
                v.wait_ge(step, steps[0])

            def modulation(L):
                bias = small[:, O_B + L * 6 * K:O_B + (L + 1) * 6 * K].rearrange("p (j k) -> p j k", j=6)
                v.wait_ge(a_free, A[("ada", L, 11)] + 1)
                then(v.tensor_tensor(mod[:, L, :, :, :], mod[:, L, :, :, :],
                                     bias.unsqueeze(3).to_broadcast([P, 6, K, 2]), ALU.add))
                for n in range(2):
                    g0 = O_G + (2 * L + n) * K
                    then(v.scalar_tensor_tensor(out=amod[:, L, n, :, :], in0=mod[:, L, 3 * n + 1, :, :], scalar=1.0,
                                                in1=small[:, g0:g0 + K].unsqueeze(2).to_broadcast([P, K, 2]),
                                                op0=ALU.add, op1=ALU.mult))
                if L == 1:
                    then(v.tensor_tensor(mod[:, L, 2, :, :], mod[:, L, 2, :, :],
                                         small[:, O_PS:O_PS + K].unsqueeze(2).to_broadcast([P, K, 2]), ALU.mult))

            def norm(i):
                L, n = divmod(i, 2)
                v.wait_ge(a_free, A[("norm", i)] + 1)
                then(v.reciprocal(std[:, :], std[:, :]))
                then(v.tensor_tensor(hT[:, :, :], xT[:, :, :], std[:, :].unsqueeze(1).to_broadcast([P, K, T]), ALU.mult))
                for k in range(K):
                    if i == 4:
                        g0 = O_G + 4 * K + k
                        last = v.tensor_scalar(hT[:, k, :], hT[:, k, :], small[:, g0:g0 + 1], None, ALU.mult)
                        continue
                    for c, (a, b) in enumerate(SEGS):
                        last = v.tensor_scalar(hT[:, k, a:b], hT[:, k, a:b], amod[:, L, n, k, c:c + 1],
                                               mod[:, L, 3 * n, k, c:c + 1], ALU.mult, ALU.add)
                last.then_inc(y_ready if i == 4 else h_ready, 1)

            def update(name, m, gate_of, ra=0, segs=SEGS):
                n = Dn[name]
                v.wait_ge(d_full, n + 1)
                for a, b in segs:
                    c = 0 if a < TS else 1
                    last = v.scalar_tensor_tensor(out=xT[:, m, a:b], in0=bankD[n % 2][:, a:b],
                                                  scalar=mod[:, gate_of[0], gate_of[1], m, c:c + 1],
                                                  in1=xT[:, m, a:b], op0=ALU.mult, op1=ALU.add)
                last.then_inc(d_free, 1)

            def attention():
                v.wait_ge(att_in, 48)

                def head_norm(s):
                    b = s % 2
                    v.wait_ge(a_free, A[("hsum", s)] + 1)
                    then(v.reciprocal(hstd[:, b, :], hstd[:, b, :]))
                    g = small[:, O_H + (s >= NH):O_H + (s >= NH) + 1]
                    dst = QT[:, s, TS:T] if s < NH else kP[:, s - NH, :]
                    v.scalar_tensor_tensor(out=dst, in0=qraw[:, b, TS:T], scalar=g, in1=hstd[:, b, TS:T],
                                           op0=ALU.mult, op1=ALU.mult)
                    v.scalar_tensor_tensor(out=qn[:, b, :], in0=qraw[:, b, 0:TS], scalar=g, in1=hstd[:, b, 0:TS],
                                           op0=ALU.mult, op1=ALU.mult).then_inc(qn_ready, 1)

                def rotary(s):
                    n = Dn[("rot", s)]
                    v.wait_ge(qn_ready, s + 1)
                    if s:
                        v.wait_ge(rope_done, s)
                    v.tensor_tensor(ropes[:, 0, :], qn[:, s % 2, :], trig[:, 0, :], ALU.mult)
                    v.wait_ge(d_full, n + 1)
                    v.tensor_tensor(ropes[:, 1, :], bankD[n % 2][:, 0:TS], trig[:, 1, :], ALU.mult).then_inc(d_free, 1)
                    v.wait_ge(d_free, n + 1)
                    dst = QT[:, s, 0:TS] if s < NH else kA[:, s - NH, P:KT * P]
                    v.tensor_tensor(dst, ropes[:, 0, :], ropes[:, 1, :], ALU.add).then_inc(rope_done, 1)

                for s in range(NH + NKV + 1):
                    if s < NH + NKV:
                        head_norm(s)
                    if s >= 1:
                        rotary(s - 1)

                def row_max(n):
                    w = KT * P if n % TILES < TILES - 1 else P
                    u = A[("score", n)]
                    if n >= 2:
                        v.wait_ge(prob_ready, n - 1)
                    v.wait_ge(a_full, u + 1)
                    then(v.tensor_reduce(smx[:, n % 2, 0:1], bankA[u % 2][:, 0:w], AX.X, ALU.max))
                    v.tensor_scalar(smx[:, n % 2, 1:2], smx[:, n % 2, 0:1], -SCALE, None, ALU.mult
                                    ).then_inc(negmax_ready, 1)

                def normalise(n):
                    w = KT * P if n % TILES < TILES - 1 else P
                    v.wait_ge(a_free, A[("score", n)] + 1)
                    then(v.reciprocal(smx[:, n % 2, 3:4], smx[:, n % 2, 2:3]))
                    v.tensor_scalar(prob[:, n % 2, 0:w], prob[:, n % 2, 0:w], smx[:, n % 2, 3:4], None, ALU.mult
                                    ).then_inc(prob_ready, 1)

                def keep_transposed(n):
                    h, t = divmod(n, TILES)
                    u = Dn[("pt", n)]
                    if t == 0 and h >= 2:
                        v.wait_ge(a_full, A[("pv", h - 2)] + 1)
                    v.wait_ge(d_full, u + 1)
                    if t < TILES - 1:
                        v.tensor_copy(PT[:, h % 2, :, t * P:(t + 1) * P],
                                      bankD[u % 2][:, 0:KT * P].rearrange("p (j q) -> p j q", q=P)).then_inc(d_free, 1)
                    else:
                        v.tensor_copy(PTp[:, h % 2, :], bankD[u % 2][:, 0:P]).then_inc(d_free, 1)

                for n in range(NH * TILES + 2):
                    if n < NH * TILES:
                        row_max(n)
                    if 1 <= n <= NH * TILES:
                        normalise(n - 1)
                    if n >= 2:
                        keep_transposed(n - 2)
                for m in range(K):
                    update(("wo", m), m, (0, 2))

            def pooling():
                v.wait_ge(inv_ready, 16)
                v.wait_ge(h_ready, 3)
                then(v.memset(pad[:, :, :, :], 0.0))
                for j, win in enumerate(WINDOWS):
                    h2 = hT[:, 2 * j:2 * j + 2, :]
                    for c, (a, b) in enumerate(SEGS):
                        last = v.tensor_copy(pad[:, 0, :, PSEG[c][0]:PSEG[c][1]], h2[:, :, a:b])
                    then(last)
                    s, w, src = 1, PW, 0
                    while s < win:
                        w -= s
                        dst = 1 if src != 1 else 2
                        then(v.tensor_tensor(pad[:, dst, :, 0:w], pad[:, src, :, 0:w], pad[:, src, :, s:s + w], ALU.add))
                        s, src = 2 * s, dst
                    for c, (a, b) in enumerate(SEGS):
                        p0 = PSEG[c][0] - win // 2
                        last = v.tensor_tensor(sq[:, 2 * j:2 * j + 2, a:b], pad[:, src, :, p0:p0 + b - a],
                                               inv[:, j, a:b].unsqueeze(1).to_broadcast([P, 2, b - a]), ALU.mult)
                    then(last)
                    v.tensor_tensor(sq[:, 2 * j:2 * j + 2, :], sq[:, 2 * j:2 * j + 2, :], h2, ALU.subtract
                                    ).then_inc(pooled_ready, 1)
                for m in range(K):
                    update(("pool", m), m, (1, 2))

            def routing(L):
                per_tile = 19
                base = steps[0]
                with v.Fori(0, TILES) as t:
                    done = [0]

                    def then_t(ins):
                        done[0] += 1
                        ins.then_inc(step, 1)
                        v.wait_ge(step, t * per_tile + (base + done[0]))
                        v.sem_inc(dve_passed, 1)

                    v.wait_ge(a_free, t * 2 + (A[("sc", L, 0, 1)] + 1))
                    v.sem_inc(dve_passed, 1)
                    for h in range(HP):
                        last = v.max(top[:, h, 0:8], sc[:, h, :])
                    then_t(last)
                    for h in range(HP):
                        v.max_index(topi[:, h, 0:8], top[:, h, 0:8], sc[:, h, :])
                    for h in range(HP):
                        last = v.match_replace(out=sc2[:, h, :], in_to_replace=top[:, h, 0:8], in_values=sc[:, h, :],
                                               imm_value=LOWEST)
                    last.then_inc(sc_used, 1)
                    v.wait_ge(sc_used, t + (L * TILES + 1))
                    v.sem_inc(dve_passed, 1)
                    for h in range(HP):
                        last = v.max(top[:, h, 8:16], sc2[:, h, :])
                    then_t(last)
                    for h in range(HP):
                        last = v.max_index(topi[:, h, 8:16], top[:, h, 8:16], sc2[:, h, :])
                    then_t(last)
                    then_t(v.tensor_copy(topf[:, :, :], topi[:, :, :]))
                    pair = top[:, :, :].rearrange("p (h c) k -> p h c k", c=2)
                    pairf = topf[:, :, :].rearrange("p (h c) k -> p h c k", c=2)
                    cand = sc2[:, :, :].rearrange("p h n -> p (h n)").rearrange("p (h a b) -> p h a b", h=PH, a=TOPK)
                    flat = sc2[:, :, :].rearrange("p h n -> p (h n)").rearrange("p (h n) -> p h n", h=PH)
                    then_t(v.tensor_tensor(cand, pair[:, :, 0, :].unsqueeze(3).to_broadcast([P, PH, TOPK, TOPK]),
                                           pair[:, :, 1, :].unsqueeze(2).to_broadcast([P, PH, TOPK, TOPK]), ALU.add))
                    for h in range(PH):
                        last = v.max(csv[:, h, 0:8], flat[:, h, :])
                    then_t(last)
                    for h in range(PH):
                        v.max_index(csi[:, h, 0:8], csv[:, h, 0:8], flat[:, h, :])
                    flat2 = mask[:, :, :].rearrange("p a b -> p (a b)").rearrange("p (h n) -> p h n", h=PH)
                    for h in range(PH):
                        last = v.match_replace(out=flat2[:, h, :], in_to_replace=csv[:, h, 0:8],
                                               in_values=flat[:, h, :], imm_value=LOWEST)
                    then_t(last)
                    for h in range(PH):
                        last = v.max(csv[:, h, 8:16], flat2[:, h, :])
                    then_t(last)
                    for h in range(PH):
                        last = v.max_index(csi[:, h, 8:16], csv[:, h, 8:16], flat2[:, h, :])
                    then_t(last)
                    ci = csi[:, :, :].rearrange("p h k -> p (h k)")
                    v.tensor_scalar(pick[:, 0, :], ci, 4, None, ALU.logical_shift_right)
                    then_t(v.tensor_scalar(pick[:, 1, :], ci, TOPK - 1, None, ALU.bitwise_and))
                    then_t(v.tensor_copy(pickf[:, :, :], pick[:, :, :]))
                    for c in range(2):
                        then_t(v.tensor_tensor(mask[:, :, :], pickf[:, c, :].unsqueeze(2).to_broadcast([P, P, TOPK]),
                                               iota[:, 0:TOPK].unsqueeze(1).to_broadcast([P, P, TOPK]), ALU.is_equal))
                        m4 = mask[:, :, :].rearrange("p (h k) a -> p h k a", h=PH)
                        then_t(v.tensor_tensor(m4, m4, pairf[:, :, c, :].unsqueeze(2).to_broadcast([P, PH, TOPK, TOPK]),
                                               ALU.mult))
                        then_t(v.tensor_reduce(i12[:, c, :], mask[:, :, :], AX.X, ALU.add))
                    then_t(v.tensor_scalar(i12[:, 0, :], i12[:, 0, :], float(L * NKEY), None, ALU.add))
                    v.scalar_tensor_tensor(out=idx[:, bass.ds(t * P, P)], in0=i12[:, 0, :], scalar=float(NKEY),
                                           in1=i12[:, 1, :], op0=ALU.mult, op1=ALU.add)
                    v.tensor_tensor(gate[:, bass.ds(t * P, P)].rearrange("p (h k) -> p h k", h=PH), csv[:, :, :],
                                    csv[:, :, 0:1].to_broadcast([P, PH, TOPK]), ALU.subtract).then_inc(step, 1)
                    done[0] += 1
                    assert done[0] == per_tile, done[0]
                steps[0] += per_tile * TILES
                v.wait_ge(step, steps[0])
                v.sem_inc(gexp_in, 1)
                v.sem_inc(idx_ready, 1)
                v.wait_ge(gexp_out, L + 1)
                g3 = gate[:, :].rearrange("p (h k) -> p h k", k=TOPK)
                then(v.tensor_reduce(gsum[:, :], g3, AX.X, ALU.add))
                then(v.reciprocal(gsum[:, :], gsum[:, :]))
                then(v.tensor_tensor(g3, g3, gsum[:, :].unsqueeze(2).to_broadcast([P, TILES * PH, TOPK]), ALU.mult))

            def experts(L):
                for t in range(TILES):
                    it0 = (L * TILES + t) * 2 * ITERS
                    v.wait_ge(a_free, A[("htok", L, t)] + 1)
                    with v.Fori(0, ITERS) as i:
                        for j in range(RING):
                            v.wait_ge(row_ready[j], i * 16 + 16 * (it0 + 1))
                            v.tensor_tensor_reduce(out=rows[:, j, :], in0=rows[:, j, :], in1=htok[:, :], scale=1.0,
                                                   scalar=0.0, op0=ALU.mult, op1=ALU.add,
                                                   accum_out=a8[:, j:j + 1]).then_inc(rows_free, 1)
                        v.wait_ge(rows_free, i * RING + (RING * (it0 + 2)))
                        v.tensor_copy(aval[:, bass.ds(i * RING, RING)], a8[:, :]).then_inc(step, 1)
                        v.wait_ge(step, i + (steps[0] + 1))
                    steps[0] += ITERS
                    v.sem_inc(u_done, 1)
                    v.memset(acc[:, :, :], 0.0)
                    v.wait_ge(gelu_done, L * TILES + t + 1)
                    then(v.tensor_tensor(actg[:, :], actg[:, :], gate[:, t * P:(t + 1) * P], ALU.mult))
                    it0 += ITERS
                    with v.Fori(0, ITERS) as i:
                        v.wait_ge(rows_free, i * RING + RING * (it0 + 1))
                        v.tensor_copy(a8[:, :], actg[:, bass.ds(i * RING, RING)]).then_inc(step, 1)
                        v.wait_ge(step, i + (steps[0] + 1))
                        for j in range(RING):
                            v.wait_ge(row_ready[j], i * 16 + 16 * (it0 + 1))
                            v.wait_ge(rows_free, i * RING + (RING * (it0 + 1) + j - 1))
                            v.scalar_tensor_tensor(out=acc[:, j % 2, :], in0=rows[:, j, :], scalar=a8[:, j:j + 1],
                                                   in1=acc[:, j % 2, :], op0=ALU.mult, op1=ALU.add
                                                   ).then_inc(rows_free, 1)
                    steps[0] += ITERS
                    v.wait_ge(rows_free, RING * (it0 + ITERS + 1))
                    v.tensor_tensor(acc[:, 0, :], acc[:, 0, :], acc[:, 1, :], ALU.add).then_inc(acc_ready, 1)
                    if L == 0 and t == 0:
                        modulation(1)
                    n = Dn[("ob", L, t)]
                    v.wait_ge(d_full, n + 1)
                    c = 0 if t < TILES - 1 else 1
                    for m in range(K):
                        last = v.scalar_tensor_tensor(out=xT[:, m, t * P:(t + 1) * P],
                                                      in0=bankD[n % 2][:, m * P:(m + 1) * P],
                                                      scalar=mod[:, L, 5, m, c:c + 1],
                                                      in1=xT[:, m, t * P:(t + 1) * P], op0=ALU.mult, op1=ALU.add)
                    last.then_inc(d_free, 1)

            then(v.memset(epsb[:, :], EPS))
            v.sem_inc(rows_free, RING)
            v.wait_ge(small_ready, 16)
            v.wait_ge(in_ready, 32)
            modulation(0)
            norm(0)
            attention()
            norm(1)
            routing(0)
            experts(0)
            norm(2)
            pooling()
            norm(3)
            routing(1)
            experts(1)
            norm(4)

        @block.tensor
        def _(pe):
            def chunk(name, cols=CH):
                n = CN[name]
                pe.wait_ge(chunk_ready[n % 2], 16 * (n // 2 + 1))
                return wch[:, n % 2, :].rearrange("p (k n) -> p k n", n=cols)

            for name, cls in ORDER:
                kind = name[0]
                n = (A if cls == "A" else Dn)[name]
                bank = (bankA if cls == "A" else bankD)[n % 2]
                full = a_full if cls == "A" else d_full
                if n >= 2:
                    pe.wait_ge(a_free if cls == "A" else d_free, n - 1)
                if kind == "ada":
                    L, j = name[1:]
                    if j == 0 and L == 0:
                        pe.wait_ge(cond_ready, 1)
                    w = chunk(name)
                    for m in range(CH // P):
                        for k in range(K):
                            last = pe.matmul(bank[:, 2 * m:2 * m + 2], w[:, k, m * P:(m + 1) * P], cs[:, k, :],
                                             start=k == 0, stop=k == K - 1)
                elif kind == "norm":
                    pe.wait_ge(sq_ready, name[1] + 1)
                    pe.wait_ge(in_ready, 32)
                    for k in range(K):
                        for a, b in SEGS:
                            last = pe.matmul(bank[:, a:b], ones, sq[:, k, a:b], start=k == 0, stop=k == K - 1)
                elif kind in ("proj", "wq"):
                    c = name[-1]
                    pe.wait_ge(h_ready, 1 if kind == "proj" else 2 + 2 * name[1])
                    w = chunk(("qkv", c // 4) if kind == "proj" else ("wq", name[1], c // 4))
                    for k in range(K):
                        for a, b in SEGS:
                            last = pe.matmul(bank[:, a:b], w[:, k, (c % 4) * P:(c % 4 + 1) * P], hT[:, k, a:b],
                                             start=k == 0, stop=k == K - 1)
                elif kind == "hsum":
                    pe.wait_ge(hsq_ready, name[1] + 1)
                    for a, b in SEGS:
                        last = pe.matmul(bank[:, a:b], ones, hsq[:, name[1] % 2, a:b], start=True, stop=True)
                elif kind == "rot":
                    pe.wait_ge(qn_ready, name[1] + 1)
                    last = pe.matmul(bank[:, 0:TS], rotp, qn[:, name[1] % 2, :], start=True, stop=True)
                elif kind == "v":
                    t = name[1]
                    w = chunk(("qkv", 2))
                    for k in range(K):
                        last = pe.matmul(bank[:, 0:NKV * HD], hT[:, k, t * P:(t + 1) * P], w[:, k, NKV * HD:CH],
                                         start=k == 0, stop=k == K - 1)
                elif kind == "score":
                    h, t = divmod(name[1], TILES)
                    if name[1] == 0:
                        pe.wait_ge(rope_done, NH + NKV)
                        pe.wait_ge(att_in, 48)
                    kv = h // (NH // NKV)
                    q = QT[:, h, t * P:(t + 1) * P]
                    if t < TILES - 1:
                        pe.matmul(bank[:, 0:512], q, kA[:, kv, 0:512], start=True, stop=True)
                        last = pe.matmul(bank[:, 512:KT * P], q, kA[:, kv, 512:KT * P], start=True, stop=True)
                    else:
                        last = pe.matmul(bank[:, 0:P], q, kP[:, kv, :], start=True, stop=True)
                elif kind == "pt":
                    pe.wait_ge(prob_ready, name[1] + 1)
                    for j in range(KT if name[1] % TILES < TILES - 1 else 1):
                        last = pe.transpose(bank[:, j * P:(j + 1) * P], prob[:, name[1] % 2, j * P:(j + 1) * P], ident)
                elif kind == "pv":
                    h = name[1]
                    kv = h // (NH // NKV)
                    pe.wait_ge(d_free, Dn[("pt", h * TILES + TILES - 1)] + 1)
                    pe.wait_ge(a_free, A[("v", TILES - 1)] + 1)
                    for j in range(KT):
                        pe.matmul(bank[:, 0:TS], vA[:, j, kv * HD:(kv + 1) * HD], PT[:, h % 2, j, :],
                                  start=j == 0, stop=j == KT - 1)
                    last = pe.matmul(bank[:, TS:T], vP[:, kv * HD:(kv + 1) * HD], PTp[:, h % 2, :], start=True, stop=True)
                elif kind == "wo":
                    m = name[1]
                    pe.wait_ge(a_free, A[("pv", NH - 1)] + 1)
                    w = chunk(("wo", m // 4))
                    for h in range(NH):
                        for a, b in SEGS:
                            last = pe.matmul(bank[:, a:b], w[:, h, (m % 4) * P:(m % 4 + 1) * P], OT[:, h, a:b],
                                             start=h == 0, stop=h == NH - 1)
                elif kind == "sc":
                    L, t, half = name[1:]
                    if t == 0 and half == 0:
                        pe.wait_ge(a_free, A[("wq", L, HP - 1)] + 1)
                        pe.wait_ge(keys_ready, 16 * (L + 1))
                    for j in range(PH):
                        c = half * PH + j
                        last = pe.matmul(bank[:, j * P:(j + 1) * P], qT[:, c, t * P:(t + 1) * P], keys[:, c, :],
                                         start=True, stop=True)
                elif kind == "htok":
                    t = name[2]
                    for m in range(K):
                        last = pe.transpose(bank[:, m * P:(m + 1) * P], hT[:, m, t * P:(t + 1) * P], ident)
                elif kind == "ob":
                    L, t = name[1:]
                    pe.wait_ge(acc_ready, L * TILES + t + 1)
                    for m in range(K):
                        last = pe.transpose(bank[:, m * P:(m + 1) * P], acc[:, 0, m * P:(m + 1) * P], ident)
                elif kind == "pool":
                    m = name[1]
                    pe.wait_ge(pooled_ready, m // 2 + 1)
                    w = chunk(("pool",), 256)
                    for k in range(2):
                        for a, b in SEGS:
                            last = pe.matmul(bank[:, a:b], w[:, 2 * (m // 2) + k, (m % 2) * P:(m % 2 + 1) * P],
                                             sq[:, 2 * (m // 2) + k, a:b], start=k == 0, stop=k == 1)
                last.then_inc(full, 1)


def shape_constants():
    const = np.zeros((P, N_CONST), np.float32)
    const[:, C_ID:C_ID + P] = np.eye(P)
    const[:, C_ONE:C_ONE + P] = 1.0
    quarter = HD // 4
    for d in range(HD):
        axis, r = divmod(d, 2 * quarter)
        src = d + quarter if r < quarter else d - quarter
        const[src, C_ROT + d] = -1.0 if r < quarter else 1.0
    const[:, C_IO:C_IO + P] = np.arange(P)
    grid = 64
    f = np.power(np.float32(10000.0), -np.arange(quarter, dtype=np.float32) / np.float32(quarter)).astype(np.float32)
    t = np.arange(TS)
    ar = (t // grid).astype(np.float32)[None] * f[:, None]
    ac = (t % grid).astype(np.float32)[None] * f[:, None]
    ang = np.concatenate([ar, ar, ac, ac])
    trig = np.stack([np.cos(ang), np.sin(ang)], 1).astype(np.float32)
    inv = np.zeros((4, T), np.float32)
    for j, w in enumerate(WINDOWS):
        for a, b in SEGS:
            s = b - a
            q = np.arange(s)
            inv[j, a:b] = 1.0 / (np.clip(q + w // 2, 0, s) - np.clip(q - w // 2, 0, s))
    return const, trig, np.broadcast_to(inv, (P, 4, T)).copy()


def kernel(x_prompt, x_sample, cache_k, cache_v, c, c_ctx, ada_w, ada_b, norm_mix_g, norm_ffn_g,
           final_norm_g, attn_w_qkv, attn_q_norm_g, attn_k_norm_g, attn_w_o, pool_w, pool_scale,
           peer_wq, peer_keys, peer_u, peer_v):
    import concourse.bacc as _bacc
    from concourse.bass_utils import run_bass_kernel_spmd as _run

    arr = {k: np.asarray(v) for k, v in locals().items() if not k.startswith("_")}
    cols = lambda a: np.ascontiguousarray(a.reshape(-1, P).T)
    rows = lambda w, n: np.ascontiguousarray(
        w.reshape(K, P, w.shape[-1] // n, n).transpose(2, 1, 0, 3)).reshape(w.shape[-1] // n, P, K * n)
    x = np.concatenate([arr["x_sample"][0], arr["x_prompt"][0]])
    xT = np.ascontiguousarray(x.T.reshape(K, P, T).transpose(1, 0, 2))
    cond = np.stack([cols(arr["c"][0]), cols(arr["c_ctx"])], 2).reshape(P, 2 * K)
    gains = [arr["norm_mix_g"][0], arr["norm_ffn_g"][0], arr["norm_mix_g"][1], arr["norm_ffn_g"][1], arr["final_norm_g"]]
    small = np.concatenate(
        [cond, cols(arr["ada_b"])] + [cols(g) for g in gains]
        + [arr["attn_q_norm_g"].T, arr["attn_k_norm_g"].T, cols(arr["pool_scale"])], 1)
    const, trig, inv = shape_constants()
    ck = np.ascontiguousarray(arr["cache_k"][0, 0].transpose(2, 1, 0))
    cv = np.ascontiguousarray(arr["cache_v"][0, 0]).reshape(P, NKV * HD)
    ada = np.stack([rows(w, CH) for w in arr["ada_w"]])
    qkv = rows(arr["attn_w_qkv"][0], CH)
    wo = rows(arr["attn_w_o"][0], CH)
    pw = np.ascontiguousarray(arr["pool_w"][0].reshape(4, 2, P, 256).transpose(2, 0, 1, 3)).reshape(P, 2048)
    wq = np.stack([rows(w, CH) for w in arr["peer_wq"]])
    keys = np.ascontiguousarray(arr["peer_keys"].reshape(DEPTH, HP, NKEY, P).transpose(0, 3, 1, 2))
    ins = dict(xT=xT, small=small, const=const, trig=trig, inv=inv, ck=ck, cv=cv, ada=ada, qkv=qkv, wo=wo, pw=pw,
               wq=wq, keys=keys, u=arr["peer_u"], v=arr["peer_v"])
    outs = dict(yT=(P, K, T), nk=(P, NKV, P), nv=(P, NKV * HD))
    nc = _bacc.Bacc("TRN2", target_bir_lowering=False, num_devices=1)
    in_aps = [nc.dram_tensor("in_" + n, a.shape, F32, kind="ExternalInput").ap() for n, a in ins.items()]
    out_aps = [nc.dram_tensor("out_" + n, s, F32, kind="ExternalOutput").ap() for n, s in outs.items()]
    build(nc, in_aps, out_aps)
    r = _run(nc, [{"in_" + n: a for n, a in ins.items()}], core_ids=[0]).results[0]
    y = np.ascontiguousarray(np.asarray(r["out_yT"]).transpose(2, 1, 0)).reshape(T, D)
    new_k = np.asarray(r["out_nk"]).transpose(2, 1, 0).reshape(1, 1, TP, NKV, HD)
    new_v = np.asarray(r["out_nv"]).reshape(1, 1, TP, NKV, HD)
    return y[None, TS:], y[None, :TS], np.ascontiguousarray(new_k), new_v
```

```python
from contextlib import ExitStack

import numpy as np
import concourse.bass as bass
from concourse import mybir

ALU = mybir.AluOpType
ACT = mybir.ActivationFunctionType
AX = mybir.AxisListType
F32 = mybir.dt.float32
U32 = mybir.dt.uint32

P = 128
D = 1024
K = D // P
DEPTH = 2
TS, TP = 512, 128
T = TS + TP
TILES = T // P
SEGS = ((0, TS), (TS, T))
NH, NKV, HD = 8, 2, 128
KT = (P + TS) // P
SCALE = HD ** -0.5
EPS = 1e-6
WINDOWS = (2, 4, 8, 16)
PH, NKEY, TOPK = 8, 128, 16
HP = 2 * PH
NE = NKEY * NKEY
CH = 512
PAD = 8
PW = PAD + TS + 2 * PAD + TP + PAD
PSEG = ((PAD, PAD + TS), (3 * PAD + TS, 3 * PAD + T))
LOWEST = -3.0e38
RING = 4
ROWS = 8
ITERS = P // ROWS
GROUP = 4
GROUPS = NKEY // GROUP
ST = TS // P
TB = 64
HOT = 4
TILE_ORDER = (TILES - 1,) + tuple(range(ST))
F32R = mybir.dt.float32r

O_C = 0
O_B = O_C + 2 * K
O_G = O_B + DEPTH * 6 * K
O_H = O_G + 5 * K
O_PS = O_H + 2
N_SMALL = O_PS + K
C_ID, C_ONE, C_ROT, C_IO = 0, P, 2 * P, 3 * P
N_CONST = 4 * P


def order_of_units():
    o = [(("ada", 0, j), "A") for j in range(12)]
    o += [(("norm", 0), "A")]
    for s in range(NH + NKV + 2):
        if s < NH + NKV:
            o.append((("proj", s), "A"))
        if 1 <= s < NH + NKV + 1:
            o.append((("hsum", s - 1), "A"))
        if s >= 2:
            o.append((("rot", s - 2), "D"))
    o += [(("v", t), "A") for t in range(TILES)]
    n_att = NH * TILES
    for n in range(n_att + 2):
        if n % 3 == 0 and n // 3 < 12:
            o.append((("ada", 1, n // 3), "A"))
        if n < n_att:
            o.append((("score", n), "A"))
        if 1 <= n <= n_att:
            o.append((("pt", n - 1), "D"))
        if n >= 2 and (n - 2) % TILES == TILES - 1:
            o.append((("pv", (n - 2) // TILES), "A"))
    o += [(("wo", m), "D") for m in range(K)]
    for L in range(DEPTH):
        if L:
            o += [(("norm", 2), "A")]
            o += [(("pool", m), "D") for m in range(K)]
        o += [(("norm", 2 * L + 1), "A")]
        o += [(("wq", L, c), "A") for c in range(HP)]
        o += [(("htok", L), "A"), (("ob", L), "D")]
    o += [(("norm", 4), "A")]
    return o


def build(nc, ins, outs):
    xT_d, small_d, const_d, trig_d, inv_d, ck_d, cv_d, ada_d, qkv_d, wo_d, pw_d, wq_d, keys_d, u_d, v_d, uT_d = ins
    y_d, nk_d, nv_d = outs

    ORDER = order_of_units()
    A, Dn = {}, {}
    for name, cls in ORDER:
        table = A if cls == "A" else Dn
        table[name] = len(table)

    chunks = [(("ada", 0, j), ("ada", 0, j)) for j in range(12)]
    chunks += [(("qkv", 0), ("proj", 3)), (("qkv", 1), ("proj", 7)), (("qkv", 2), ("v", TILES - 1))]
    chunks += [(("ada", 1, j), ("ada", 1, j)) for j in range(12)]
    chunks += [(("wo", 0), ("wo", 3)), (("wo", 1), ("wo", 7))]
    chunks += [(("wq", 0, i), ("wq", 0, 4 * i + 3)) for i in range(4)]
    chunks += [(("pool",), ("pool", K - 1))]
    chunks += [(("wq", 1, i), ("wq", 1, 4 * i + 3)) for i in range(4)]
    CN = {c[0]: n for n, c in enumerate(chunks)}

    with ExitStack() as ctx:
        def sb(name, shape, dt=F32, where=None):
            return (where or ctx).enter_context(nc.sbuf_tensor(name, shape, dt))

        def sem(name):
            return ctx.enter_context(nc.semaphore(name))

        bankA = [ctx.enter_context(nc.psum_tensor(f"bankA{i}", [P, 1024], F32)) for i in range(2)]
        bankD = [ctx.enter_context(nc.psum_tensor(f"bankD{i}", [P, 1024], F32)) for i in range(2)]

        gates_d = nc.dram_tensor("gates_scratch", [TS // TB, P, NKEY, TB], F32).ap()

        xT = sb("xT", [P, K, T])
        hT = sb("hT", [P, K, T])
        small = sb("small", [P, N_SMALL])
        const = sb("const", [P, N_CONST])
        epsb = sb("epsb", [P, 1])
        cs = sb("cs", [P, K, 2])
        mod = sb("mod", [P, DEPTH, 6, K, 2])
        amod = sb("amod", [P, DEPTH, 2, K, 2])
        idx = sb("idx", [P, P], U32)
        gate = sb("gate", [P, P])
        aval = sb("aval", [P, P])
        actg = sb("actg", [P, P])
        a8 = sb("a8", [P, ROWS])
        idxc = sb("idxc", [P, 2, RING], U32)
        ident = const[:, C_ID:C_ID + P]
        ones = const[:, C_ONE:C_ONE + P]
        rotp = const[:, C_ROT:C_ROT + P]
        iota = const[:, C_IO:C_IO + P]

        with ExitStack() as front:
            std = sb("std", [P, T], where=front)
            qT = sb("qT", [P, HP, T], where=front)
            keys = sb("keys", [P, HP, NKEY], where=front)
            QT, OT = qT[:, 0:NH, :], qT[:, NH:2 * NH, :]
            with ExitStack() as wa:
                wch = sb("wch", [P, 2, K * CH], where=wa)
                sq = sb("sq", [P, K, T], where=wa)
                PT = sq[:, :, :].rearrange("p k t -> p (k t)").rearrange("p (b j q) -> p b j q", b=2, j=KT)
                with ExitStack() as att:
                    trig = sb("trig", [P, 2, TS], where=att)
                    kA = sb("kA", [P, NKV, KT * P], where=att)
                    kP = sb("kP", [P, NKV, P], where=att)
                    vA = sb("vA", [P, KT, NKV * HD], where=att)
                    vP = sb("vP", [P, NKV * HD], where=att)
                    PTp = sb("PTp", [P, 2, P], where=att)
                    prob = sb("prob", [P, 2, KT * P], where=att)
                    qraw = sb("qraw", [P, 2, T], where=att)
                    hsq = sb("hsq", [P, 2, T], where=att)
                    hstd = sb("hstd", [P, 2, T], where=att)
                    qn = sb("qn", [P, 2, TS], where=att)
                    ropes = sb("ropes", [P, 2, TS], where=att)
                    smx = sb("smx", [P, 2, 4], where=att)
                with ExitStack() as pl:
                    inv = sb("inv", [P, 4, T], where=pl)
                    pad = sb("pad", [P, 3, 2, PW], where=pl)
            with ExitStack() as rt:
                sc = sb("sc", [P, HP, NKEY], where=rt)
                sc2 = sb("sc2", [P, HP, NKEY], where=rt)
                mask = sb("mask", [P, PH * TOPK, TOPK], where=rt)
                top = sb("top", [P, HP, TOPK], where=rt)
                topi = sb("topi", [P, HP, TOPK], U32, where=rt)
                topf = sb("topf", [P, HP, TOPK], where=rt)
                csv = sb("csv", [P, PH, TOPK], where=rt)
                csi = sb("csi", [P, PH, TOPK], U32, where=rt)
                pick = sb("pick", [P, 2, PH * TOPK], U32, where=rt)
                pickf = sb("pickf", [P, 2, PH * TOPK], where=rt)
                i12 = sb("i12", [P, 2, PH * TOPK], where=rt)
                gt = sb("gt", [P, PH, TOPK], where=rt)
                gsum = sb("gsum", [P, PH], where=rt)
                pickT = sb("pickT", [P, 3, P], where=rt)
                hot = sb("hot", [P, 2, 2, HOT, P], where=rt)
                gbuf = sb("gbuf", [P, 2, NKEY, TB], where=rt)
        with ExitStack() as dn:
            hh = sb("hh", [P, K, TS], F32R, where=dn)
            hl = sb("hl", [P, K, TS], F32R, where=dn)
            uraw = sb("uraw", [P, 2, D], where=dn)
            uh = sb("uh", [P, 2, D], F32R, where=dn)
            ul = sb("ul", [P, 2, D], F32R, where=dn)
            vraw = sb("vraw", [P, 2, D], where=dn)
            vh = sb("vh", [P, GROUP, D], F32R, where=dn)
            vl = sb("vl", [P, GROUP, D], F32R, where=dn)
            wt = sb("wt", [P, 2, TS], where=dn)
            wh = sb("wh", [P, GROUP, TS], F32R, where=dn)
            wl = sb("wl", [P, GROUP, TS], F32R, where=dn)
            gp = sb("gp", [P, 2, TS // TB, 2, TB], where=dn)
            rows = sb("rows", [P, RING, D], where=dn)
            htok = sb("htok", [P, D], where=dn)
            acc = sb("acc", [P, 2, D], where=dn)
        abank = [bankA[i][:, 0:TS] for i in range(2)]
        obank = [bankD[i // 2][:, 512 * (i % 2):512 * (i % 2) + TS] for i in range(4)]

        small_ready = sem("small_ready")
        in_ready = sem("in_ready")
        att_in = sem("att_in")
        keys_ready = sem("keys_ready")
        inv_ready = sem("inv_ready")
        chunk_ready = [sem(f"chunk_ready{i}") for i in range(2)]
        row_ready = [sem(f"row_ready{i}") for i in range(RING)]
        a_full = sem("a_full")
        a_free = sem("a_free")
        d_full = sem("d_full")
        d_free = sem("d_free")
        cond_ready = sem("cond_ready")
        sq_ready = sem("sq_ready")
        h_ready = sem("h_ready")
        hsq_ready = sem("hsq_ready")
        qn_ready = sem("qn_ready")
        rope_done = sem("rope_done")
        negmax_ready = sem("negmax_ready")
        prob_ready = sem("prob_ready")
        pooled_ready = sem("pooled_ready")
        sc_full = sem("sc_full")
        sc_copied = sem("sc_copied")
        sc_used = sem("sc_used")
        gexp_in = sem("gexp_in")
        gexp_out = sem("gexp_out")
        routed = sem("routed")
        pickT_full = sem("pickT_full")
        pickT_ready = sem("pickT_ready")
        hot_ready = sem("hot_ready")
        g_full = sem("g_full")
        g_out = sem("g_out")
        stored = [sem(f"stored{i}") for i in range(2)]
        split_h = sem("split_h")
        h_split = sem("h_split")
        uraw_ready = [sem(f"uraw_ready{i}") for i in range(2)]
        vraw_ready = [sem(f"vraw_ready{i}") for i in range(2)]
        gp_ready = [sem(f"gp_ready{i}") for i in range(2)]
        uh_ready = sem("uh_ready")
        ul_ready = sem("ul_ready")
        vh_ready = sem("vh_ready")
        vl_ready = sem("vl_ready")
        a_done = sem("a_done")
        gelu_ready = sem("gelu_ready")
        wm_ready = sem("wm_ready")
        wh_ready = sem("wh_ready")
        wl_ready = sem("wl_ready")
        out_full = sem("out_full")
        acc_done = sem("acc_done")
        dense_begun = sem("dense_begun")
        act_passed = sem("act_passed")
        idx_ready = sem("idx_ready")
        idx_copied = sem("idx_copied")
        rows_free = sem("rows_free")
        u_done = sem("u_done")
        gelu_done = sem("gelu_done")
        acc_ready = sem("acc_ready")
        step = sem("step")
        y_ready = sem("y_ready")
        dve_passed = sem("dve_passed")
        pool_passed = sem("pool_passed")
        out_done = sem("out_done")

        block = ctx.enter_context(nc.Block())

        @block.sync
        def _(sp):
            def source(name):
                if name[0] == "ada":
                    return ada_d[name[1], name[2]]
                if name[0] == "qkv":
                    return qkv_d[name[1]]
                if name[0] == "wo":
                    return wo_d[name[1]]
                if name[0] == "wq":
                    return wq_d[name[1], name[2]]
                return pw_d

            def store_gates(L):
                for b in range(TS // TB):
                    n = L * (TS // TB) + b
                    sp.wait_ge(g_out, (n + 1) * (TB // HOT) + 2)
                    sp.dma_start(gates_d[b], gbuf[:, b % 2, :, :]).then_inc(stored[b % 2], 16)

            def expert_loads(L):
                def load_u(q, e, slot):
                    sp.wait_ge(ul_ready, q + 1)
                    sp.dma_start(uraw[:, slot, :], uT_d[L, bass.ds(e, 1)].rearrange("o p n -> (o p) n")).then_inc(uraw_ready[slot], 16)

                def group(g, last=False):
                    for c in range(GROUP):
                        e = g * GROUP + c
                        q = e + L * NKEY
                        sp.wait_ge(vl_ready, q + 1)
                        sp.dma_start(vraw[:, c % 2, :], v_d[L, bass.ds(e * P, P), :] if not last
                                     else v_d[L, e * P:(e + 1) * P, :]).then_inc(vraw_ready[c % 2], 16)
                        if c % 2 == 0:
                            s2 = c // 2
                            sp.wait_ge(wm_ready, q + 2)
                            src = gates_d[:, :, bass.ds(e, 2), :] if not last else gates_d[:, :, e:e + 2, :]
                            sp.dma_start(gp[:, s2, :, :, :].rearrange("p b i t -> p b (i t)"),
                                         src.rearrange("b p i t -> p b (i t)")).then_inc(gp_ready[s2], 16)
                        if not (last and c >= 2):
                            load_u(q + 2, e + 2, c % 2)

                sp.wait_ge(dense_begun, L + 1)
                load_u(L * NKEY, 0, 0)
                load_u(L * NKEY + 1, 1, 1)
                with sp.Fori(0, GROUPS - 1) as g:
                    group(g)
                group(GROUPS - 1, last=True)

            for i in range(2):
                sp.sem_inc(stored[i], 16)
            sp.dma_start(small[:, :], small_d).then_inc(small_ready, 16)
            for n, (name, last) in enumerate(chunks):
                if n >= 2 and name not in (("pool",), ("wq", 1, 0)):
                    u = chunks[n - 2][1]
                    if u in A:
                        sp.wait_ge(a_full, A[u] + 1)
                    else:
                        sp.wait_ge(d_full, Dn[u] + 1)
                src = source(name)
                sp.dma_start(wch[:, n % 2, 0:src.shape[1]], src).then_inc(chunk_ready[n % 2], 16)
                if n == 1:
                    sp.dma_start(const[:, :], const_d).then_inc(in_ready, 16)
                    sp.dma_start(xT[:, :, :], xT_d).then_inc(in_ready, 16)
                    sp.dma_start(trig[:, :, :], trig_d).then_inc(att_in, 16)
                    sp.dma_start(kA[:, :, 0:P], ck_d).then_inc(att_in, 16)
                    sp.dma_start(vA[:, 0, :], cv_d).then_inc(att_in, 16)
                    sp.dma_start(keys[:, :, :], keys_d[0]).then_inc(keys_ready, 16)
                if name == ("wo", 1):
                    sp.wait_ge(rope_done, NH + NKV)
                    sp.dma_start(nk_d, kP[:, :, :]).then_inc(out_done, 16)
                    sp.wait_ge(a_free, A[("v", TILES - 1)] + 1)
                    sp.dma_start(nv_d, vP[:, :]).then_inc(out_done, 16)
                if name == ("wq", 0, 3) or name == ("wq", 1, 3):
                    L = name[1]
                    store_gates(L)
                    expert_loads(L)
                    if L == 0:
                        sp.wait_ge(d_full, Dn[("ob", 0)] + 1)
                        sp.dma_start(keys[:, :, :], keys_d[1]).then_inc(keys_ready, 16)
                        sp.dma_start(inv[:, :, :], inv_d).then_inc(inv_ready, 16)
            sp.wait_ge(y_ready, 1)
            sp.dma_start(y_d, hT[:, :, :]).then_inc(out_done, 16)
            sp.wait_ge(out_done, 48)

        @block.gpsimd
        def _(pool):
            for L in range(DEPTH):
                pool.wait_ge(idx_ready, L + 1)
                pool.wait_ge(dense_begun, L + 1)
                for stage, table in enumerate((u_d, v_d)):
                    with pool.Fori(0, ITERS) as i:
                        it = i + (L * 2 + stage) * ITERS
                        for g in range(ROWS // RING):
                            pool.wait_ge(rows_free, it * ROWS + (g * RING + 1))
                            pool.tensor_copy(idxc[:, g, :], idx[:, bass.ds(i * ROWS + g * RING, RING)]
                                             ).then_inc(idx_copied, 1)
                            pool.wait_ge(idx_copied, it * 2 + (g + 1))
                            pool.sem_inc(pool_passed, 1)
                            for j in range(RING):
                                pool.wait_ge(rows_free, it * ROWS + (g * RING + j + 1))
                                pool.sem_inc(pool_passed, 1)
                                pool.indirect_dma_start(
                                    out=rows[:, j, :], out_offset=None, in_=table.rearrange("l e d -> (l e) d"),
                                    in_offset=bass.IndirectOffsetOnAxis(ap=idxc[:, g, j:j + 1], axis=0),
                                ).then_inc(row_ready[j], 16)

        @block.scalar
        def _(act):
            act.wait_ge(small_ready, 16)
            act.activation(cs[:, :, :].rearrange("p k c -> p (k c)"), small[:, O_C:O_C + 2 * K],
                           ACT.Silu).then_inc(cond_ready, 1)
            def route_copies(L):
                def scores(i):
                    n = L * TILES + i
                    if n:
                        act.wait_ge(sc_used, n)
                    for half in range(2):
                        act.wait_ge(sc_full, 2 * n + half + 1)
                        act.copy(sc[:, half * PH:(half + 1) * PH, :],
                                 bankA[half][:, :].rearrange("p (h n) -> p h n", n=NKEY)).then_inc(sc_copied, 1)

                scores(0)
                for i in range(TILES):
                    act.wait_ge(gexp_in, L * TILES + i + 1)
                    act.activation(gt[:, :, :], gt[:, :, :], ACT.Exp).then_inc(gexp_out, 1)
                    if i + 1 < TILES:
                        scores(i + 1)
                    for half in range(2 if i else 0):
                        n0 = ((L * ST + i - 1) * 2 + half) * (TB // HOT)
                        act.wait_ge(stored[half], 16 * (L * ST + i))
                        with act.Fori(0, TB // HOT // 2) as k:
                            for b in range(2):
                                act.wait_ge(g_full, k * 2 + (n0 + b + 3))
                                act.copy(gbuf[:, half, :, bass.ds(k * 2 * HOT + b * HOT, HOT)],
                                         bankD[1][:, b * 512:(b + 1) * 512].rearrange("p (t i) -> p i t", i=NKEY)
                                         ).then_inc(g_out, 1)

            def experts(L):
                def split_u(q, b):
                    act.wait_ge(a_done, q + 1)
                    act.sem_inc(act_passed, 1)
                    act.wait_ge(uraw_ready[b], q * 8 + (16 - 8 * b))
                    act.copy(uh[:, b, :], uraw[:, b, :]).then_inc(uh_ready, 1)

                def group(g, last=False):
                    for c in range(GROUP):
                        q = g * GROUP + (c + L * NKEY)
                        act.wait_ge(out_full, g * K + (L * GROUPS * K + 1))
                        act.sem_inc(act_passed, 1)
                        act.wait_ge(vraw_ready[c % 2], q * 8 + (16 - 8 * (c % 2)))
                        act.copy(vh[:, c, :], vraw[:, c % 2, :]).then_inc(vh_ready, 1)
                        act.wait_ge(wl_ready, q + 1)
                        act.sem_inc(act_passed, 1)
                        act.wait_ge(a_done, q + 3)
                        act.activation(wt[:, c % 2, :], abank[c % 2], ACT.Gelu).then_inc(gelu_ready, 1)
                        act.wait_ge(wm_ready, q + 5)
                        act.copy(wh[:, c, :], wt[:, c % 2, :]).then_inc(wh_ready, 1)
                        if not (last and c >= 2):
                            split_u(q + 2, c % 2)

                split_u(L * NKEY, 0)
                split_u(L * NKEY + 1, 1)
                with act.Fori(0, ITERS) as g:
                    group(g)
                act.wait_ge(u_done, L + 1)
                act.activation(actg[:, :], aval[:, :], ACT.Gelu).then_inc(gelu_done, 1)
                with act.Fori(ITERS, GROUPS - 1) as g:
                    group(g)
                group(GROUPS - 1, last=True)

            act.sem_inc(gelu_ready, 2)
            act.sem_inc(g_out, 2)
            for name, cls in ORDER:
                if cls != "A":
                    continue
                n = A[name]
                bank = bankA[n % 2]
                kind = name[0]
                if kind == "norm":
                    i = name[1]
                    if i == 0:
                        act.wait_ge(in_ready, 32)
                        act.wait_ge(step, 1)
                    else:
                        before = {1: ("wo", K - 1), 2: ("ob", 0), 3: ("pool", K - 1), 4: ("ob", 1)}[i]
                        act.wait_ge(d_free, Dn[before] + 1)
                    act.activation(sq[:, :, :], xT[:, :, :], ACT.Square).then_inc(sq_ready, 1)
                    act.wait_ge(a_full, n + 1)
                    act.activation(std[:, :], bank[:, 0:T], ACT.Sqrt, bias=epsb[:, 0:1],
                                   scale=1.0 / D).then_inc(a_free, 1)
                    continue
                if kind in ("proj", "hsum") and name[1] >= 2:
                    act.wait_ge(qn_ready, name[1] - 1)
                if kind == "score":
                    act.wait_ge(negmax_ready, name[1] + 1)
                    if name[1] >= 2:
                        act.wait_ge(d_full, Dn[("pt", name[1] - 2)] + 1)
                if kind == "htok":
                    route_copies(name[1])
                    act.wait_ge(dense_begun, name[1] + 1)
                    act.copy(hh[:, :, :], hT[:, :, 0:TS]).then_inc(split_h, 1)
                act.wait_ge(a_full, n + 1)
                if kind == "ada":
                    L, j = name[1:]
                    act.copy(mod[:, L, j // 2, 4 * (j % 2):4 * (j % 2) + 4, :],
                             bank[:, 0:8].rearrange("p (m c) -> p m c", c=2)).then_inc(a_free, 1)
                elif kind == "proj":
                    b = name[1] % 2
                    act.activation(hsq[:, b, :], bank[:, 0:T], ACT.Square).then_inc(hsq_ready, 1)
                    act.copy(qraw[:, b, :], bank[:, 0:T]).then_inc(a_free, 1)
                elif kind == "hsum":
                    act.activation(hstd[:, name[1] % 2, :], bank[:, 0:T], ACT.Sqrt, bias=epsb[:, 0:1],
                                   scale=1.0 / HD).then_inc(a_free, 1)
                elif kind == "v":
                    dst = vA[:, 1 + name[1], :] if name[1] < TILES - 1 else vP[:, :]
                    act.copy(dst, bank[:, 0:NKV * HD]).then_inc(a_free, 1)
                elif kind == "score":
                    b = name[1] % 2
                    w = KT * P if name[1] % TILES < TILES - 1 else P
                    act.activation(prob[:, b, 0:w], bank[:, 0:w], ACT.Exp, bias=smx[:, b, 1:2],
                                   scale=SCALE, accum_out=smx[:, b, 2:3]).then_inc(a_free, 1)
                elif kind == "pv":
                    act.copy(OT[:, name[1], :], bank[:, 0:T]).then_inc(a_free, 1)
                elif kind == "wq":
                    act.copy(qT[:, name[2], :], bank[:, 0:T]).then_inc(a_free, 1)
                elif kind == "htok":
                    act.copy(htok[:, :], bank[:, :]).then_inc(a_free, 1)
                    experts(name[1])

        @block.vector
        def _(v):
            steps = [0]

            def then(ins):
                steps[0] += 1
                ins.then_inc(step, 1)
                v.wait_ge(step, steps[0])

            def modulation(L):
                bias = small[:, O_B + L * 6 * K:O_B + (L + 1) * 6 * K].rearrange("p (j k) -> p j k", j=6)
                v.wait_ge(a_free, A[("ada", L, 11)] + 1)
                then(v.tensor_tensor(mod[:, L, :, :, :], mod[:, L, :, :, :],
                                     bias.unsqueeze(3).to_broadcast([P, 6, K, 2]), ALU.add))
                for n in range(2):
                    g0 = O_G + (2 * L + n) * K
                    then(v.scalar_tensor_tensor(out=amod[:, L, n, :, :], in0=mod[:, L, 3 * n + 1, :, :], scalar=1.0,
                                                in1=small[:, g0:g0 + K].unsqueeze(2).to_broadcast([P, K, 2]),
                                                op0=ALU.add, op1=ALU.mult))
                if L == 1:
                    then(v.tensor_tensor(mod[:, L, 2, :, :], mod[:, L, 2, :, :],
                                         small[:, O_PS:O_PS + K].unsqueeze(2).to_broadcast([P, K, 2]), ALU.mult))

            def norm(i):
                L, n = divmod(i, 2)
                v.wait_ge(a_free, A[("norm", i)] + 1)
                then(v.reciprocal(std[:, :], std[:, :]))
                then(v.tensor_tensor(hT[:, :, :], xT[:, :, :], std[:, :].unsqueeze(1).to_broadcast([P, K, T]), ALU.mult))
                for k in range(K):
                    if i == 4:
                        g0 = O_G + 4 * K + k
                        last = v.tensor_scalar(hT[:, k, :], hT[:, k, :], small[:, g0:g0 + 1], None, ALU.mult)
                        continue
                    for c, (a, b) in enumerate(SEGS):
                        last = v.tensor_scalar(hT[:, k, a:b], hT[:, k, a:b], amod[:, L, n, k, c:c + 1],
                                               mod[:, L, 3 * n, k, c:c + 1], ALU.mult, ALU.add)
                last.then_inc(y_ready if i == 4 else h_ready, 1)

            def update(name, m, gate_of, ra=0, segs=SEGS):
                n = Dn[name]
                v.wait_ge(d_full, n + 1)
                for a, b in segs:
                    c = 0 if a < TS else 1
                    last = v.scalar_tensor_tensor(out=xT[:, m, a:b], in0=bankD[n % 2][:, a:b],
                                                  scalar=mod[:, gate_of[0], gate_of[1], m, c:c + 1],
                                                  in1=xT[:, m, a:b], op0=ALU.mult, op1=ALU.add)
                last.then_inc(d_free, 1)

            def attention():
                v.wait_ge(att_in, 48)

                def head_norm(s):
                    b = s % 2
                    v.wait_ge(a_free, A[("hsum", s)] + 1)
                    then(v.reciprocal(hstd[:, b, :], hstd[:, b, :]))
                    g = small[:, O_H + (s >= NH):O_H + (s >= NH) + 1]
                    dst = QT[:, s, TS:T] if s < NH else kP[:, s - NH, :]
                    v.scalar_tensor_tensor(out=dst, in0=qraw[:, b, TS:T], scalar=g, in1=hstd[:, b, TS:T],
                                           op0=ALU.mult, op1=ALU.mult)
                    v.scalar_tensor_tensor(out=qn[:, b, :], in0=qraw[:, b, 0:TS], scalar=g, in1=hstd[:, b, 0:TS],
                                           op0=ALU.mult, op1=ALU.mult).then_inc(qn_ready, 1)

                def rotary(s):
                    n = Dn[("rot", s)]
                    v.wait_ge(qn_ready, s + 1)
                    if s:
                        v.wait_ge(rope_done, s)
                    v.tensor_tensor(ropes[:, 0, :], qn[:, s % 2, :], trig[:, 0, :], ALU.mult)
                    v.wait_ge(d_full, n + 1)
                    v.tensor_tensor(ropes[:, 1, :], bankD[n % 2][:, 0:TS], trig[:, 1, :], ALU.mult).then_inc(d_free, 1)
                    v.wait_ge(d_free, n + 1)
                    dst = QT[:, s, 0:TS] if s < NH else kA[:, s - NH, P:KT * P]
                    v.tensor_tensor(dst, ropes[:, 0, :], ropes[:, 1, :], ALU.add).then_inc(rope_done, 1)

                for s in range(NH + NKV + 1):
                    if s < NH + NKV:
                        head_norm(s)
                    if s >= 1:
                        rotary(s - 1)

                def row_max(n):
                    w = KT * P if n % TILES < TILES - 1 else P
                    u = A[("score", n)]
                    if n >= 2:
                        v.wait_ge(prob_ready, n - 1)
                    v.wait_ge(a_full, u + 1)
                    then(v.tensor_reduce(smx[:, n % 2, 0:1], bankA[u % 2][:, 0:w], AX.X, ALU.max))
                    v.tensor_scalar(smx[:, n % 2, 1:2], smx[:, n % 2, 0:1], -SCALE, None, ALU.mult
                                    ).then_inc(negmax_ready, 1)

                def normalise(n):
                    w = KT * P if n % TILES < TILES - 1 else P
                    v.wait_ge(a_free, A[("score", n)] + 1)
                    then(v.reciprocal(smx[:, n % 2, 3:4], smx[:, n % 2, 2:3]))
                    v.tensor_scalar(prob[:, n % 2, 0:w], prob[:, n % 2, 0:w], smx[:, n % 2, 3:4], None, ALU.mult
                                    ).then_inc(prob_ready, 1)

                def keep_transposed(n):
                    h, t = divmod(n, TILES)
                    u = Dn[("pt", n)]
                    if t == 0 and h >= 2:
                        v.wait_ge(a_full, A[("pv", h - 2)] + 1)
                    v.wait_ge(d_full, u + 1)
                    if t < TILES - 1:
                        v.tensor_copy(PT[:, h % 2, :, t * P:(t + 1) * P],
                                      bankD[u % 2][:, 0:KT * P].rearrange("p (j q) -> p j q", q=P)).then_inc(d_free, 1)
                    else:
                        v.tensor_copy(PTp[:, h % 2, :], bankD[u % 2][:, 0:P]).then_inc(d_free, 1)

                for n in range(NH * TILES + 2):
                    if n < NH * TILES:
                        row_max(n)
                    if 1 <= n <= NH * TILES:
                        normalise(n - 1)
                    if n >= 2:
                        keep_transposed(n - 2)
                for m in range(K):
                    update(("wo", m), m, (0, 2))

            def pooling():
                v.wait_ge(inv_ready, 16)
                v.wait_ge(h_ready, 3)
                then(v.memset(pad[:, :, :, :], 0.0))
                for j, win in enumerate(WINDOWS):
                    h2 = hT[:, 2 * j:2 * j + 2, :]
                    for c, (a, b) in enumerate(SEGS):
                        last = v.tensor_copy(pad[:, 0, :, PSEG[c][0]:PSEG[c][1]], h2[:, :, a:b])
                    then(last)
                    s, w, src = 1, PW, 0
                    while s < win:
                        w -= s
                        dst = 1 if src != 1 else 2
                        then(v.tensor_tensor(pad[:, dst, :, 0:w], pad[:, src, :, 0:w], pad[:, src, :, s:s + w], ALU.add))
                        s, src = 2 * s, dst
                    for c, (a, b) in enumerate(SEGS):
                        p0 = PSEG[c][0] - win // 2
                        last = v.tensor_tensor(sq[:, 2 * j:2 * j + 2, a:b], pad[:, src, :, p0:p0 + b - a],
                                               inv[:, j, a:b].unsqueeze(1).to_broadcast([P, 2, b - a]), ALU.mult)
                    then(last)
                    v.tensor_tensor(sq[:, 2 * j:2 * j + 2, :], sq[:, 2 * j:2 * j + 2, :], h2, ALU.subtract
                                    ).then_inc(pooled_ready, 1)
                for m in range(K):
                    update(("pool", m), m, (1, 2))

            def routing(L):
                per_tile = 24
                base = steps[0]
                done = [0]

                def route(i, t):
                    done[0] = 0

                    def wait_t():
                        v.wait_ge(step, i * per_tile + (base + done[0]))
                        v.sem_inc(dve_passed, 1)

                    def then_t(ins):
                        done[0] += 1
                        ins.then_inc(step, 1)
                        wait_t()

                    v.wait_ge(sc_copied, i * 2 + (L * TILES * 2 + 2))
                    v.sem_inc(dve_passed, 1)
                    for h in range(HP):
                        last = v.max(top[:, h, 0:8], sc[:, h, :])
                    then_t(last)
                    for h in range(HP):
                        v.max_index(topi[:, h, 0:8], top[:, h, 0:8], sc[:, h, :])
                    for h in range(HP):
                        last = v.match_replace(out=sc2[:, h, :], in_to_replace=top[:, h, 0:8], in_values=sc[:, h, :],
                                               imm_value=LOWEST)
                    last.then_inc(sc_used, 1)
                    v.wait_ge(sc_used, i + (L * TILES + 1))
                    v.sem_inc(dve_passed, 1)
                    for h in range(HP):
                        last = v.max(top[:, h, 8:16], sc2[:, h, :])
                    then_t(last)
                    for h in range(HP):
                        last = v.max_index(topi[:, h, 8:16], top[:, h, 8:16], sc2[:, h, :])
                    then_t(last)
                    then_t(v.tensor_copy(topf[:, :, :], topi[:, :, :]))
                    pair = top[:, :, :].rearrange("p (h c) k -> p h c k", c=2)
                    pairf = topf[:, :, :].rearrange("p (h c) k -> p h c k", c=2)
                    flat = sc2[:, :, :].rearrange("p h n -> p (h n)").rearrange("p (h n) -> p h n", h=PH)
                    cand = sc2[:, :, :].rearrange("p h n -> p (h n)").rearrange("p (h a b) -> p h a b", h=PH, a=TOPK)
                    then_t(v.tensor_tensor(cand, pair[:, :, 0, :].unsqueeze(3).to_broadcast([P, PH, TOPK, TOPK]),
                                           pair[:, :, 1, :].unsqueeze(2).to_broadcast([P, PH, TOPK, TOPK]), ALU.add))
                    for h in range(PH):
                        last = v.max(csv[:, h, 0:8], flat[:, h, :])
                    then_t(last)
                    for h in range(PH):
                        v.max_index(csi[:, h, 0:8], csv[:, h, 0:8], flat[:, h, :])
                    flat2 = mask[:, :, :].rearrange("p a b -> p (a b)").rearrange("p (h n) -> p h n", h=PH)
                    for h in range(PH):
                        last = v.match_replace(out=flat2[:, h, :], in_to_replace=csv[:, h, 0:8],
                                               in_values=flat[:, h, :], imm_value=LOWEST)
                    then_t(last)
                    for h in range(PH):
                        last = v.max(csv[:, h, 8:16], flat2[:, h, :])
                    then_t(last)
                    v.tensor_tensor(gt[:, :, :], csv[:, :, :], csv[:, :, 0:1].to_broadcast([P, PH, TOPK]),
                                    ALU.subtract).then_inc(gexp_in, 1)
                    for h in range(PH):
                        last = v.max_index(csi[:, h, 8:16], csv[:, h, 8:16], flat2[:, h, :])
                    then_t(last)
                    ci = csi[:, :, :].rearrange("p h k -> p (h k)")
                    v.tensor_scalar(pick[:, 0, :], ci, 4, None, ALU.logical_shift_right)
                    then_t(v.tensor_scalar(pick[:, 1, :], ci, TOPK - 1, None, ALU.bitwise_and))
                    then_t(v.tensor_copy(pickf[:, :, :], pick[:, :, :]))
                    for c in range(2):
                        then_t(v.tensor_tensor(mask[:, :, :], pickf[:, c, :].unsqueeze(2).to_broadcast([P, P, TOPK]),
                                               iota[:, 0:TOPK].unsqueeze(1).to_broadcast([P, P, TOPK]), ALU.is_equal))
                        m4 = mask[:, :, :].rearrange("p (h k) a -> p h k a", h=PH)
                        then_t(v.tensor_tensor(m4, m4, pairf[:, :, c, :].unsqueeze(2).to_broadcast([P, PH, TOPK, TOPK]),
                                               ALU.mult))
                        then_t(v.tensor_reduce(i12[:, c, :], mask[:, :, :], AX.X, ALU.add))
                    v.wait_ge(gexp_out, i + (L * TILES + 1))
                    then_t(v.tensor_reduce(gsum[:, :], gt[:, :, :], AX.X, ALU.add))
                    then_t(v.reciprocal(gsum[:, :], gsum[:, :]))
                    v.tensor_tensor(gt[:, :, :], gt[:, :, :], gsum[:, :].unsqueeze(2).to_broadcast([P, PH, TOPK]),
                                    ALU.mult).then_inc(routed, 1)

                if L == 0:
                    v.wait_ge(out_done, 32)
                route(0, TILES - 1)
                n_route = done[0]
                v.wait_ge(routed, L * TILES + 1)
                then_p = [v.tensor_copy(gate[:, :], gt[:, :, :].rearrange("p h k -> p (h k)")),
                          v.tensor_scalar(i12[:, 0, :], i12[:, 0, :], float(L * NKEY), None, ALU.add)]
                then_p[1].then_inc(step, 1)
                v.wait_ge(step, base + n_route + 1)
                v.scalar_tensor_tensor(out=idx[:, :], in0=i12[:, 0, :], scalar=float(NKEY), in1=i12[:, 1, :],
                                       op0=ALU.mult, op1=ALU.add).then_inc(idx_ready, 1)
                v.wait_ge(idx_ready, L + 1)
                base += n_route + 1 - n_route
                per_tile = n_route

                with v.Fori(1, TILES) as i:
                    route(i, i)
                    v.wait_ge(pickT_full, i + L * ST)
                    v.tensor_copy(pickT[:, :, :], bankD[0][:, 0:3 * P].rearrange("p (j t) -> p j t", j=3)
                                  ).then_inc(pickT_ready, 1)
                    v.wait_ge(pickT_ready, i + L * ST)
                    v.sem_inc(dve_passed, 1)
                    with v.Fori(0, P // HOT // 2) as k:
                        for b in range(2):
                            n = (i - 1 + L * ST) * (P // HOT) + k * 2 + b
                            t0 = k * 2 * HOT + b * HOT
                            v.wait_ge(g_full, n + 1)
                            v.tensor_tensor(hot[:, b, 1, :, :],
                                            pickT[:, 1, bass.ds(t0, HOT)].unsqueeze(2).to_broadcast([P, HOT, P]),
                                            iota.unsqueeze(1).to_broadcast([P, HOT, P]), ALU.is_equal)
                            for j in range(HOT):
                                last = v.tensor_scalar(hot[:, b, 0, j, :], iota, pickT[:, 0, bass.ds(t0 + j, 1)],
                                                       pickT[:, 2, bass.ds(t0 + j, 1)], ALU.is_equal, ALU.mult)
                            last.then_inc(hot_ready, 1)
                    v.wait_ge(hot_ready, (i + L * ST) * (P // HOT))
                    v.sem_inc(dve_passed, 1)
                steps[0] = base + per_tile * TILES
                v.wait_ge(step, steps[0])

            def experts(L):
                def split_u(q, b):
                    v.wait_ge(uh_ready, q + 1)
                    v.tensor_tensor(ul[:, b, :], uraw[:, b, :], uh[:, b, :].bitcast(F32), ALU.subtract
                                    ).then_inc(ul_ready, 1)

                def u_row(g, r):
                    n = (g + L * 2 * ITERS) * (ROWS // RING) + r // RING
                    v.wait_ge(row_ready[r % RING], n * 16 + 16)
                    v.tensor_tensor_reduce(out=rows[:, r % RING, :], in0=rows[:, r % RING, :], in1=htok[:, :],
                                           scale=1.0, scalar=0.0, op0=ALU.mult, op1=ALU.add,
                                           accum_out=a8[:, r:r + 1]).then_inc(rows_free, 1)

                def v_row(g, r):
                    it = g - ITERS + (L * 2 + 1) * ITERS
                    v.wait_ge(row_ready[r % RING], (it * (ROWS // RING) + r // RING) * 16 + 16)
                    v.wait_ge(rows_free, it * ROWS + (RING + r - 1))
                    v.scalar_tensor_tensor(out=acc[:, r % 2, :], in0=rows[:, r % RING, :], scalar=a8[:, r:r + 1],
                                           in1=acc[:, r % 2, :], op0=ALU.mult, op1=ALU.add).then_inc(rows_free, 1)

                def group(g, row, last=False):
                    for c in range(GROUP):
                        q = g * GROUP + (c + L * NKEY)
                        v.wait_ge(gelu_ready, q + 3)
                        v.wait_ge(gp_ready[c // 2], (g + L * GROUPS) * 16 + 16)
                        w3 = wt[:, c % 2, :].rearrange("p (b t) -> p b t", t=TB)
                        v.tensor_tensor(w3, w3, gp[:, c // 2, :, c % 2, :], ALU.mult).then_inc(wm_ready, 1)
                        v.wait_ge(vh_ready, q + 1)
                        v.tensor_tensor(vl[:, c, :], vraw[:, c % 2, :], vh[:, c, :].bitcast(F32), ALU.subtract
                                        ).then_inc(vl_ready, 1)
                        v.wait_ge(wh_ready, q + 1)
                        v.tensor_tensor(wl[:, c, :], wt[:, c % 2, :], wh[:, c, :].bitcast(F32), ALU.subtract
                                        ).then_inc(wl_ready, 1)
                        if not (last and c >= 2):
                            split_u(q + 2, c % 2)
                    for m in range(K):
                        row(g, m)
                        r = g * K + (m + L * GROUPS * K)
                        v.wait_ge(acc_done, r + 1)
                        v.wait_ge(out_full, r + 2)
                        v.tensor_tensor(hT[:, m, 0:TS], obank[m % 4], hT[:, m, 0:TS], ALU.add).then_inc(acc_done, 1)

                v.wait_ge(g_out, (L + 1) * ST * (P // HOT) + 2)
                for i in range(2):
                    v.wait_ge(stored[i], 16 * ((L + 1) * ST + 1))
                v.sem_inc(dense_begun, 1)
                v.wait_ge(split_h, L + 1)
                v.tensor_tensor(hl[:, :, :], hT[:, :, 0:TS], hh[:, :, :].bitcast(F32), ALU.subtract).then_inc(h_split, 1)
                v.wait_ge(h_split, L + 1)
                v.memset(hT[:, :, 0:TS], 0.0)
                then(v.memset(acc[:, :, :], 0.0))
                v.wait_ge(a_free, A[("htok", L)] + 1)
                split_u(L * NKEY, 0)
                split_u(L * NKEY + 1, 1)
                with v.Fori(0, ITERS) as g:
                    group(g, u_row)
                    v.wait_ge(rows_free, g * ROWS + (L * 2 * ITERS * ROWS + ROWS + RING))
                    v.tensor_copy(aval[:, bass.ds(g * ROWS, ROWS)], a8[:, :]).then_inc(step, 1)
                    v.wait_ge(step, g + (steps[0] + 1))
                    v.sem_inc(dve_passed, 1)
                steps[0] += ITERS
                v.sem_inc(u_done, 1)
                v.wait_ge(gelu_done, L + 1)
                then(v.tensor_tensor(actg[:, :], actg[:, :], gate[:, :], ALU.mult))

                def v_group(g, last=False):
                    it = g - ITERS + (L * 2 + 1) * ITERS
                    v.wait_ge(rows_free, it * ROWS + RING)
                    i0 = (g - ITERS) * ROWS
                    v.tensor_copy(a8[:, :], actg[:, i0:i0 + ROWS] if last else actg[:, bass.ds(i0, ROWS)]
                                  ).then_inc(step, 1)
                    v.wait_ge(step, g - ITERS + (steps[0] + 1))
                    v.sem_inc(dve_passed, 1)
                    group(g, v_row, last)

                with v.Fori(ITERS, GROUPS - 1) as g:
                    v_group(g)
                v_group(GROUPS - 1, last=True)
                steps[0] += ITERS
                v.wait_ge(rows_free, RING + (L + 1) * 2 * P)
                v.tensor_tensor(acc[:, 0, :], acc[:, 0, :], acc[:, 1, :], ALU.add).then_inc(acc_ready, 1)
                v.wait_ge(acc_done, (L + 1) * GROUPS * K + K)
                for m in range(K):
                    v.scalar_tensor_tensor(out=xT[:, m, 0:TS], in0=hT[:, m, 0:TS], scalar=mod[:, L, 5, m, 0:1],
                                           in1=xT[:, m, 0:TS], op0=ALU.mult, op1=ALU.add)
                n = Dn[("ob", L)]
                v.wait_ge(d_full, n + 1)
                for m in range(K):
                    last = v.scalar_tensor_tensor(out=xT[:, m, TS:T], in0=bankD[n % 2][:, m * P:(m + 1) * P],
                                                  scalar=mod[:, L, 5, m, 1:2], in1=xT[:, m, TS:T],
                                                  op0=ALU.mult, op1=ALU.add)
                last.then_inc(d_free, 1)

            then(v.memset(epsb[:, :], EPS))
            v.sem_inc(rows_free, RING)
            v.sem_inc(ul_ready, 2)
            v.sem_inc(vl_ready, 2)
            v.sem_inc(wl_ready, 2)
            v.sem_inc(wm_ready, 4)
            v.sem_inc(acc_done, K)
            v.wait_ge(small_ready, 16)
            v.wait_ge(in_ready, 32)
            modulation(0)
            norm(0)
            attention()
            modulation(1)
            norm(1)
            routing(0)
            experts(0)
            norm(2)
            pooling()
            norm(3)
            routing(1)
            experts(1)
            norm(4)

        @block.tensor
        def _(pe):
            def chunk(name, cols=CH):
                n = CN[name]
                pe.wait_ge(chunk_ready[n % 2], 16 * (n // 2 + 1))
                return wch[:, n % 2, :].rearrange("p (k n) -> p k n", n=cols)

            def routes(L):
                pe.wait_ge(a_free, A[("wq", L, HP - 1)] + 1)
                pe.wait_ge(d_free, Dn[("wo", K - 1) if L == 0 else ("pool", K - 1)] + 1)
                pe.wait_ge(keys_ready, 16 * (L + 1))

                def scores(i):
                    t = TILE_ORDER[i]
                    for half in range(2):
                        if L or i:
                            pe.wait_ge(sc_copied, 2 * (L * TILES + i - 1) + half + 1)
                        for j in range(PH):
                            c = half * PH + j
                            last = pe.matmul(bankA[half][:, j * P:(j + 1) * P], qT[:, c, t * P:(t + 1) * P],
                                             keys[:, c, :], start=True, stop=True)
                        last.then_inc(sc_full, 1)

                scores(0)
                scores(1)
                for i in range(1, TILES):
                    pe.wait_ge(routed, L * TILES + i + 1)
                    if L * ST + i > 1:
                        pe.wait_ge(pickT_ready, L * ST + i - 1)
                    pe.transpose(bankD[0][:, 0:P], i12[:, 0, :], ident)
                    pe.transpose(bankD[0][:, P:2 * P], i12[:, 1, :], ident)
                    pe.transpose(bankD[0][:, 2 * P:3 * P], gt[:, :, :].rearrange("p h k -> p (h k)"), ident
                                 ).then_inc(pickT_full, 1)
                    if i + 1 < TILES:
                        scores(i + 1)
                    with pe.Fori(0, P // HOT // 2) as k:
                        for b in range(2):
                            n = k * 2 + ((L * ST + i - 1) * (P // HOT) + b)
                            pe.wait_ge(g_out, n + 1)
                            pe.wait_ge(hot_ready, n + 1)
                            for j in range(HOT):
                                last = pe.matmul(bankD[1][:, b * 512 + j * P:b * 512 + (j + 1) * P],
                                                 hot[:, b, 1, j, :], hot[:, b, 0, j, :], start=True, stop=True)
                            last.then_inc(g_full, 1)
                pe.wait_ge(sc_copied, 2 * TILES * (L + 1))
                pe.wait_ge(g_out, (L + 1) * ST * (P // HOT) + 2)

            def experts(L):
                def group(g):
                    for c in range(GROUP):
                        q = g * GROUP + (c + L * NKEY)
                        pe.wait_ge(gelu_ready, q + 1)
                        pe.wait_ge(ul_ready, q + 3)
                        bank = abank[c % 2]
                        for k in range(K):
                            hi, lo = uh[:, c % 2, k * P:(k + 1) * P], ul[:, c % 2, k * P:(k + 1) * P]
                            pe.matmul(bank, hi, hh[:, k, :], start=k == 0, stop=False)
                            pe.matmul(bank, hi, hl[:, k, :], start=False, stop=False)
                            last = pe.matmul(bank, lo, hh[:, k, :], start=False, stop=k == K - 1)
                        last.then_inc(a_done, 1)

                    def out(m, chunks):
                        for c in chunks:
                            hi, lo = vh[:, c, m * P:(m + 1) * P], vl[:, c, m * P:(m + 1) * P]
                            pe.matmul(obank[m % 4], hi, wh[:, c, :], start=c == 0, stop=False)
                            pe.matmul(obank[m % 4], hi, wl[:, c, :], start=False, stop=False)
                            last = pe.matmul(obank[m % 4], lo, wh[:, c, :], start=False, stop=c == GROUP - 1)
                        return last

                    q = g * GROUP + L * NKEY
                    r = g * K + L * GROUPS * K
                    pe.wait_ge(wl_ready, q + (GROUP - 1 + 2))
                    pe.wait_ge(vl_ready, q + (GROUP - 1 + 2))
                    for m in range(2):
                        pe.wait_ge(acc_done, r + (m + 1 + K - 4))
                        out(m, range(GROUP - 1))
                    pe.wait_ge(wl_ready, q + (GROUP + 2))
                    pe.wait_ge(vl_ready, q + (GROUP + 2))
                    for m in range(2):
                        out(m, (GROUP - 1,)).then_inc(out_full, 1)
                    for m in range(2, K):
                        pe.wait_ge(acc_done, r + (m + 1 + K - 4))
                        last = out(m, range(GROUP))
                        if m < K - 1:
                            last.then_inc(out_full, 1)
                    last.then_inc(out_full, 1)

                pe.wait_ge(h_split, L + 1)
                pe.wait_ge(split_h, L + 1)
                with pe.Fori(0, GROUPS) as g:
                    group(g)
                pe.wait_ge(acc_done, (L + 1) * GROUPS * K + K)

            pe.sem_inc(g_full, 2)
            pe.sem_inc(a_done, 2)
            pe.sem_inc(out_full, 1)
            for name, cls in ORDER:
                kind = name[0]
                n = (A if cls == "A" else Dn)[name]
                bank = (bankA if cls == "A" else bankD)[n % 2]
                full = a_full if cls == "A" else d_full
                if kind == "htok":
                    routes(name[1])
                if kind == "ob":
                    experts(name[1])
                if n >= 2:
                    pe.wait_ge(a_free if cls == "A" else d_free, n - 1)
                if kind == "ada":
                    L, j = name[1:]
                    if j == 0 and L == 0:
                        pe.wait_ge(cond_ready, 1)
                    w = chunk(name)
                    for m in range(CH // P):
                        for k in range(K):
                            last = pe.matmul(bank[:, 2 * m:2 * m + 2], w[:, k, m * P:(m + 1) * P], cs[:, k, :],
                                             start=k == 0, stop=k == K - 1)
                elif kind == "norm":
                    pe.wait_ge(sq_ready, name[1] + 1)
                    pe.wait_ge(in_ready, 32)
                    for k in range(K):
                        for a, b in SEGS:
                            last = pe.matmul(bank[:, a:b], ones, sq[:, k, a:b], start=k == 0, stop=k == K - 1)
                elif kind in ("proj", "wq"):
                    c = name[-1]
                    pe.wait_ge(h_ready, 1 if kind == "proj" else 2 + 2 * name[1])
                    w = chunk(("qkv", c // 4) if kind == "proj" else ("wq", name[1], c // 4))
                    for k in range(K):
                        for a, b in SEGS:
                            last = pe.matmul(bank[:, a:b], w[:, k, (c % 4) * P:(c % 4 + 1) * P], hT[:, k, a:b],
                                             start=k == 0, stop=k == K - 1)
                elif kind == "hsum":
                    pe.wait_ge(hsq_ready, name[1] + 1)
                    for a, b in SEGS:
                        last = pe.matmul(bank[:, a:b], ones, hsq[:, name[1] % 2, a:b], start=True, stop=True)
                elif kind == "rot":
                    pe.wait_ge(qn_ready, name[1] + 1)
                    last = pe.matmul(bank[:, 0:TS], rotp, qn[:, name[1] % 2, :], start=True, stop=True)
                elif kind == "v":
                    t = name[1]
                    w = chunk(("qkv", 2))
                    for k in range(K):
                        last = pe.matmul(bank[:, 0:NKV * HD], hT[:, k, t * P:(t + 1) * P], w[:, k, NKV * HD:CH],
                                         start=k == 0, stop=k == K - 1)
                elif kind == "score":
                    h, t = divmod(name[1], TILES)
                    if name[1] == 0:
                        pe.wait_ge(rope_done, NH + NKV)
                        pe.wait_ge(att_in, 48)
                    kv = h // (NH // NKV)
                    q = QT[:, h, t * P:(t + 1) * P]
                    if t < TILES - 1:
                        pe.matmul(bank[:, 0:512], q, kA[:, kv, 0:512], start=True, stop=True)
                        last = pe.matmul(bank[:, 512:KT * P], q, kA[:, kv, 512:KT * P], start=True, stop=True)
                    else:
                        last = pe.matmul(bank[:, 0:P], q, kP[:, kv, :], start=True, stop=True)
                elif kind == "pt":
                    pe.wait_ge(prob_ready, name[1] + 1)
                    for j in range(KT if name[1] % TILES < TILES - 1 else 1):
                        last = pe.transpose(bank[:, j * P:(j + 1) * P], prob[:, name[1] % 2, j * P:(j + 1) * P], ident)
                elif kind == "pv":
                    h = name[1]
                    kv = h // (NH // NKV)
                    pe.wait_ge(d_free, Dn[("pt", h * TILES + TILES - 1)] + 1)
                    pe.wait_ge(a_free, A[("v", TILES - 1)] + 1)
                    for j in range(KT):
                        pe.matmul(bank[:, 0:TS], vA[:, j, kv * HD:(kv + 1) * HD], PT[:, h % 2, j, :],
                                  start=j == 0, stop=j == KT - 1)
                    last = pe.matmul(bank[:, TS:T], vP[:, kv * HD:(kv + 1) * HD], PTp[:, h % 2, :], start=True, stop=True)
                elif kind == "wo":
                    m = name[1]
                    pe.wait_ge(a_free, A[("pv", NH - 1)] + 1)
                    w = chunk(("wo", m // 4))
                    for h in range(NH):
                        for a, b in SEGS:
                            last = pe.matmul(bank[:, a:b], w[:, h, (m % 4) * P:(m % 4 + 1) * P], OT[:, h, a:b],
                                             start=h == 0, stop=h == NH - 1)
                elif kind == "htok":
                    for m in range(K):
                        last = pe.transpose(bank[:, m * P:(m + 1) * P], hT[:, m, TS:T], ident)
                elif kind == "ob":
                    pe.wait_ge(acc_ready, name[1] + 1)
                    for m in range(K):
                        last = pe.transpose(bank[:, m * P:(m + 1) * P], acc[:, 0, m * P:(m + 1) * P], ident)
                elif kind == "pool":
                    m = name[1]
                    pe.wait_ge(pooled_ready, m // 2 + 1)
                    w = chunk(("pool",), 256)
                    for k in range(2):
                        for a, b in SEGS:
                            last = pe.matmul(bank[:, a:b], w[:, 2 * (m // 2) + k, (m % 2) * P:(m % 2 + 1) * P],
                                             sq[:, 2 * (m // 2) + k, a:b], start=k == 0, stop=k == 1)
                last.then_inc(full, 1)


def shape_constants():
    const = np.zeros((P, N_CONST), np.float32)
    const[:, C_ID:C_ID + P] = np.eye(P)
    const[:, C_ONE:C_ONE + P] = 1.0
    quarter = HD // 4
    for d in range(HD):
        axis, r = divmod(d, 2 * quarter)
        src = d + quarter if r < quarter else d - quarter
        const[src, C_ROT + d] = -1.0 if r < quarter else 1.0
    const[:, C_IO:C_IO + P] = np.arange(P)
    grid = 64
    f = np.power(np.float32(10000.0), -np.arange(quarter, dtype=np.float32) / np.float32(quarter)).astype(np.float32)
    t = np.arange(TS)
    ar = (t // grid).astype(np.float32)[None] * f[:, None]
    ac = (t % grid).astype(np.float32)[None] * f[:, None]
    ang = np.concatenate([ar, ar, ac, ac])
    trig = np.stack([np.cos(ang), np.sin(ang)], 1).astype(np.float32)
    inv = np.zeros((4, T), np.float32)
    for j, w in enumerate(WINDOWS):
        for a, b in SEGS:
            s = b - a
            q = np.arange(s)
            inv[j, a:b] = 1.0 / (np.clip(q + w // 2, 0, s) - np.clip(q - w // 2, 0, s))
    return const, trig, np.broadcast_to(inv, (P, 4, T)).copy()


def kernel(x_prompt, x_sample, cache_k, cache_v, c, c_ctx, ada_w, ada_b, norm_mix_g, norm_ffn_g,
           final_norm_g, attn_w_qkv, attn_q_norm_g, attn_k_norm_g, attn_w_o, pool_w, pool_scale,
           peer_wq, peer_keys, peer_u, peer_v):
    import concourse.bacc as _bacc
    from concourse.bass_utils import run_bass_kernel_spmd as _run

    arr = {k: np.asarray(v) for k, v in locals().items() if not k.startswith("_")}
    cols = lambda a: np.ascontiguousarray(a.reshape(-1, P).T)
    rows = lambda w, n: np.ascontiguousarray(
        w.reshape(K, P, w.shape[-1] // n, n).transpose(2, 1, 0, 3)).reshape(w.shape[-1] // n, P, K * n)
    x = np.concatenate([arr["x_sample"][0], arr["x_prompt"][0]])
    xT = np.ascontiguousarray(x.T.reshape(K, P, T).transpose(1, 0, 2))
    cond = np.stack([cols(arr["c"][0]), cols(arr["c_ctx"])], 2).reshape(P, 2 * K)
    gains = [arr["norm_mix_g"][0], arr["norm_ffn_g"][0], arr["norm_mix_g"][1], arr["norm_ffn_g"][1], arr["final_norm_g"]]
    small = np.concatenate(
        [cond, cols(arr["ada_b"])] + [cols(g) for g in gains]
        + [arr["attn_q_norm_g"].T, arr["attn_k_norm_g"].T, cols(arr["pool_scale"])], 1)
    const, trig, inv = shape_constants()
    ck = np.ascontiguousarray(arr["cache_k"][0, 0].transpose(2, 1, 0))
    cv = np.ascontiguousarray(arr["cache_v"][0, 0]).reshape(P, NKV * HD)
    ada = np.stack([rows(w, CH) for w in arr["ada_w"]])
    qkv = rows(arr["attn_w_qkv"][0], CH)
    wo = rows(arr["attn_w_o"][0], CH)
    pw = np.ascontiguousarray(arr["pool_w"][0].reshape(4, 2, P, 256).transpose(2, 0, 1, 3)).reshape(P, 2048)
    wq = np.stack([rows(w, CH) for w in arr["peer_wq"]])
    keys = np.ascontiguousarray(arr["peer_keys"].reshape(DEPTH, HP, NKEY, P).transpose(0, 3, 1, 2))
    uT = np.ascontiguousarray(arr["peer_u"].reshape(DEPTH, NKEY, P, K, P).transpose(0, 1, 4, 3, 2)
                              ).reshape(DEPTH, NKEY, P, D)
    ins = dict(xT=xT, small=small, const=const, trig=trig, inv=inv, ck=ck, cv=cv, ada=ada, qkv=qkv, wo=wo, pw=pw,
               wq=wq, keys=keys, u=arr["peer_u"], v=arr["peer_v"], uT=uT)
    outs = dict(yT=(P, K, T), nk=(P, NKV, P), nv=(P, NKV * HD))
    nc = _bacc.Bacc("TRN2", target_bir_lowering=False, num_devices=1)
    in_aps = [nc.dram_tensor("in_" + n, a.shape, F32, kind="ExternalInput").ap() for n, a in ins.items()]
    out_aps = [nc.dram_tensor("out_" + n, s, F32, kind="ExternalOutput").ap() for n, s in outs.items()]
    build(nc, in_aps, out_aps)
    r = _run(nc, [{"in_" + n: a for n, a in ins.items()}], core_ids=[0]).results[0]
    y = np.ascontiguousarray(np.asarray(r["out_yT"]).transpose(2, 1, 0)).reshape(T, D)
    new_k = np.asarray(r["out_nk"]).transpose(2, 1, 0).reshape(1, 1, TP, NKV, HD)
    new_v = np.asarray(r["out_nv"]).reshape(1, 1, TP, NKV, HD)
    return y[None, TS:], y[None, :TS], np.ascontiguousarray(new_k), new_v
```

```python
from contextlib import ExitStack

import numpy as np
import concourse.bass as bass
from concourse import mybir

ALU = mybir.AluOpType
ACT = mybir.ActivationFunctionType
AX = mybir.AxisListType
F32 = mybir.dt.float32
U32 = mybir.dt.uint32

P = 128
D = 1024
K = D // P
DEPTH = 2
TS, TP = 512, 128
T = TS + TP
TILES = T // P
SEGS = ((0, TS), (TS, T))
NH, NKV, HD = 8, 2, 128
KT = (P + TS) // P
SCALE = HD ** -0.5
EPS = 1e-6
WINDOWS = (2, 4, 8, 16)
PH, NKEY, TOPK = 8, 128, 16
HP = 2 * PH
NE = NKEY * NKEY
CH = 512
NADA = 6 * D // CH
NMIX = 2 * D // CH
PAD = 8
PW = PAD + TS + 2 * PAD + TP + PAD
PSEG = ((PAD, PAD + TS), (3 * PAD + TS, 3 * PAD + T))
LOWEST = -3.0e38
RING = 4
ROWS = 8
ITERS = P // ROWS
GROUP = 4
GROUPS = NKEY // GROUP
ST = TS // P
TB = 64
HOT = 4
SLOTS = 4
TILE_ORDER = (TILES - 1,) + tuple(range(ST))
F32R = mybir.dt.float32r

O_C = 0
O_B = O_C + 2 * K
O_G = O_B + DEPTH * 6 * K
O_H = O_G + 5 * K
O_PS = O_H + 2
N_SMALL = O_PS + K
C_ID, C_ONE, C_ROT, C_IO = 0, P, 2 * P, 3 * P
N_CONST = 4 * P


ADA_FIRST = [(0, j) for j in range(NMIX)]
ADA_LATER = [(0, j) for j in range(NMIX, NADA)] + [(1, j) for j in range(NADA)]


def order_of_units():
    def ada(some, i):
        return ([(("ada",) + some[i], "A")] if i < len(some) else []) + ([(("adat",) + some[i - 1], "A")] if i else [])

    o = []
    for i in range(NMIX + 1):
        o += ada(ADA_FIRST, i)
    o += [(("norm", 0), "A")]
    for s in range(NH + NKV + 2):
        if s < NH + NKV:
            o.append((("proj", s), "A"))
        if 1 <= s < NH + NKV + 1:
            o.append((("hsum", s - 1), "A"))
        if s >= 2:
            o.append((("rot", s - 2), "D"))
    o += [(("v", t), "A") for t in range(TILES)]
    n_att = NH * TILES
    for n in range(n_att + 3):
        if n < n_att:
            o.append((("score", n), "A"))
        if n // 2 < len(ADA_LATER):
            o.append((("adat" if n % 2 else "ada",) + ADA_LATER[n // 2], "A"))
        if 2 <= n < n_att + 2:
            o.append((("pt", n - 2), "D"))
        if n >= 3 and (n - 3) % TILES == TILES - 1:
            o.append((("pv", (n - 3) // TILES), "A"))
    o += [(("wo", m), "D") for m in range(K)]
    for L in range(DEPTH):
        if L:
            o += [(("norm", 2), "A")]
            o += [(("pool", m), "D") for m in range(K)]
        o += [(("norm", 2 * L + 1), "A")]
        o += [(("wq", L, c), "A") for c in range(HP)]
        o += [(("htok", L), "A"), (("ob", L), "D")]
    o += [(("norm", 4), "A")]
    return o


def build(nc, ins, outs):
    xT_d, small_d, const_d, trig_d, inv_d, ck_d, cv_d, ada_d, qkv_d, wo_d, pw_d, wq_d, keys_d, u_d, v_d, uT_d = ins
    y_d, nk_d, nv_d = outs

    ORDER = order_of_units()
    A, Dn = {}, {}
    for name, cls in ORDER:
        table = A if cls == "A" else Dn
        table[name] = len(table)

    chunks = [(("ada",) + a, ("ada",) + a) for a in ADA_FIRST]
    chunks += [(("qkv", 0), ("proj", 3)), (("qkv", 1), ("proj", 7)), (("qkv", 2), ("v", TILES - 1))]
    chunks += [(("ada",) + a, ("ada",) + a) for a in ADA_LATER]
    chunks += [(("wo", 0), ("wo", 3)), (("wo", 1), ("wo", 7))]
    chunks += [(("wq", 0, i), ("wq", 0, 4 * i + 3)) for i in range(4)]
    chunks += [(("pool",), ("pool", K - 1))]
    chunks += [(("wq", 1, i), ("wq", 1, 4 * i + 3)) for i in range(4)]
    CN = {c[0]: n for n, c in enumerate(chunks)}

    with ExitStack() as ctx:
        def sb(name, shape, dt=F32, where=None):
            return (where or ctx).enter_context(nc.sbuf_tensor(name, shape, dt))

        def sem(name):
            return ctx.enter_context(nc.semaphore(name))

        bankA = [ctx.enter_context(nc.psum_tensor(f"bankA{i}", [P, 1024], F32)) for i in range(2)]
        bankD = [ctx.enter_context(nc.psum_tensor(f"bankD{i}", [P, 1024], F32)) for i in range(2)]

        gates_d = nc.dram_tensor("gates_scratch", [TS // TB, P, NKEY, TB], F32).ap()

        xT = sb("xT", [P, K, T])
        hT = sb("hT", [P, K, T])
        small = sb("small", [P, N_SMALL])
        const = sb("const", [P, N_CONST])
        epsb = sb("epsb", [P, 1])
        cs = sb("cs", [P, K, 2])
        mod = sb("mod", [P, DEPTH, 6, K, 2])
        amod = sb("amod", [P, DEPTH, 2, K, 2])
        idx = sb("idx", [P, P], U32)
        gate = sb("gate", [P, P])
        aval = sb("aval", [P, P])
        actg = sb("actg", [P, P])
        a8 = sb("a8", [P, ROWS])
        idxc = sb("idxc", [P, 2, RING], U32)
        ident = const[:, C_ID:C_ID + P]
        ones = const[:, C_ONE:C_ONE + P]
        rotp = const[:, C_ROT:C_ROT + P]
        iota = const[:, C_IO:C_IO + P]

        with ExitStack() as front:
            std = sb("std", [P, T], where=front)
            keys = sb("keys", [P, HP, NKEY], where=front)
            adar = sb("adar", [2, 2, CH], where=front)
            with ExitStack() as att:
                trig = sb("trig", [P, 2, TS], where=att)
                kA = sb("kA", [P, NKV, KT * P], where=att)
                kP = sb("kP", [P, NKV, P], where=att)
                vA = sb("vA", [P, KT, NKV * HD], where=att)
                vP = sb("vP", [P, NKV * HD], where=att)
                PTp = sb("PTp", [P, 2, P], where=att)
                prob = sb("prob", [P, 2, KT * P], where=att)
                qraw = sb("qraw", [P, 2, T], where=att)
                hsq = sb("hsq", [P, 2, T], where=att)
                hstd = sb("hstd", [P, 2, T], where=att)
                qn = sb("qn", [P, 2, TS], where=att)
                ropes = sb("ropes", [P, 2, TS], where=att)
                smx = sb("smx", [P, 2, 4], where=att)
                with ExitStack() as wide:
                    qT = sb("qT", [P, HP, T], where=wide)
                    wch = sb("wch", [P, 2, K * CH], where=wide)
                    sq = sb("sq", [P, K, T], where=wide)
                with ExitStack() as gb:
                    pickT = sb("pickT", [P, 3, P], where=gb)
                    hot = sb("hot", [P, SLOTS, 2, HOT, P], where=gb)
                    gbuf = sb("gbuf", [P, 2, NKEY, TB], where=gb)
            QT, OT = qT[:, 0:NH, :], qT[:, NH:2 * NH, :]
            PT = sq[:, :, :].rearrange("p k t -> p (k t)").rearrange("p (b j q) -> p b j q", b=2, j=KT)
            with ExitStack() as rt:
                sc = sb("sc", [P, 2, TILES, NKEY], where=rt)
                sc2 = sb("sc2", [P, 2, TILES, NKEY], where=rt)
                cand = sb("cand", [P, TILES, TOPK * TOPK], where=rt)
                cand2 = sb("cand2", [P, TILES, TOPK * TOPK], where=rt)
                mask = sb("mask", [P, 2, TILES, TOPK, TOPK], where=rt)
                top = sb("top", [P, 2, TILES, TOPK], where=rt)
                topi = sb("topi", [P, 2, TILES, TOPK], U32, where=rt)
                topf = sb("topf", [P, 2, TILES, TOPK], where=rt)
                csv = sb("csv", [P, TILES, TOPK], where=rt)
                csi = sb("csi", [P, TILES, TOPK], U32, where=rt)
                pick = sb("pick", [P, 2, TILES * TOPK], U32, where=rt)
                pickf = sb("pickf", [P, 2, TILES * TOPK], where=rt)
                i12 = sb("i12", [P, TILES, 2, PH * TOPK], where=rt)
                gt = sb("gt", [P, TILES, PH * TOPK], where=rt)
                gsum = sb("gsum", [P, TILES * PH], where=rt)
            with ExitStack() as pl:
                inv = sb("inv", [P, 4, T], where=pl)
                pad = sb("pad", [P, 3, 2, PW], where=pl)
        with ExitStack() as dn:
            hh = sb("hh", [P, K, TS], F32R, where=dn)
            hl = sb("hl", [P, K, TS], F32R, where=dn)
            uraw = sb("uraw", [P, 2, D], where=dn)
            uh = sb("uh", [P, 2, D], F32R, where=dn)
            ul = sb("ul", [P, 2, D], F32R, where=dn)
            vraw = sb("vraw", [P, 2, D], where=dn)
            vh = sb("vh", [P, GROUP, D], F32R, where=dn)
            vl = sb("vl", [P, GROUP, D], F32R, where=dn)
            wt = sb("wt", [P, 2, TS], where=dn)
            wh = sb("wh", [P, GROUP, TS], F32R, where=dn)
            wl = sb("wl", [P, GROUP, TS], F32R, where=dn)
            gp = sb("gp", [P, 2, TS // TB, 2, TB], where=dn)
            rows = sb("rows", [P, RING, D], where=dn)
            htok = sb("htok", [P, D], where=dn)
            acc = sb("acc", [P, 2, D], where=dn)
        abank = [bankA[i][:, 0:TS] for i in range(2)]
        obank = [bankD[i // 2][:, 512 * (i % 2):512 * (i % 2) + TS] for i in range(4)]

        small_ready = sem("small_ready")
        in_ready = sem("in_ready")
        att_in = sem("att_in")
        keys_ready = sem("keys_ready")
        inv_ready = sem("inv_ready")
        chunk_ready = [sem(f"chunk_ready{i}") for i in range(2)]
        row_ready = [sem(f"row_ready{i}") for i in range(RING)]
        a_full = sem("a_full")
        a_free = sem("a_free")
        d_full = sem("d_full")
        d_free = sem("d_free")
        cond_ready = sem("cond_ready")
        x_ready = sem("x_ready")
        sq_ready = sem("sq_ready")
        scaled = sem("scaled")
        h_ready = sem("h_ready")
        hsq_ready = sem("hsq_ready")
        qn_ready = sem("qn_ready")
        rope_done = sem("rope_done")
        negmax_ready = sem("negmax_ready")
        prob_ready = sem("prob_ready")
        pooled_ready = sem("pooled_ready")
        sc_full = sem("sc_full")
        sc_copied = sem("sc_copied")
        mask_ready = sem("mask_ready")
        mask_scaled = sem("mask_scaled")
        mask_done = sem("mask_done")
        sc_used = sem("sc_used")
        gexp_in = sem("gexp_in")
        gexp_out = sem("gexp_out")
        routed = sem("routed")
        pickT_full = sem("pickT_full")
        pickT_ready = sem("pickT_ready")
        hot_ready = sem("hot_ready")
        hotg_ready = sem("hotg_ready")
        g_full = sem("g_full")
        g_out = sem("g_out")
        stored = [sem(f"stored{i}") for i in range(2)]
        split_h = sem("split_h")
        h_split = sem("h_split")
        uraw_ready = [sem(f"uraw_ready{i}") for i in range(2)]
        vraw_ready = [sem(f"vraw_ready{i}") for i in range(2)]
        gp_ready = [sem(f"gp_ready{i}") for i in range(2)]
        uh_ready = sem("uh_ready")
        ul_ready = sem("ul_ready")
        vh_ready = sem("vh_ready")
        vl_ready = sem("vl_ready")
        a_done = sem("a_done")
        gelu_ready = sem("gelu_ready")
        wm_ready = sem("wm_ready")
        wh_ready = sem("wh_ready")
        wl_ready = sem("wl_ready")
        out_full = sem("out_full")
        acc_done = sem("acc_done")
        dense_begun = sem("dense_begun")
        act_passed = sem("act_passed")
        idx_ready = sem("idx_ready")
        idx_copied = sem("idx_copied")
        rows_free = sem("rows_free")
        u_done = sem("u_done")
        gelu_done = sem("gelu_done")
        acc_ready = sem("acc_ready")
        step = sem("step")
        y_ready = sem("y_ready")
        dve_passed = sem("dve_passed")
        pool_passed = sem("pool_passed")
        out_done = sem("out_done")

        block = ctx.enter_context(nc.Block())

        @block.sync
        def _(sp):
            def source(name):
                if name[0] == "ada":
                    return ada_d[name[1], name[2]]
                if name[0] == "qkv":
                    return qkv_d[name[1]]
                if name[0] == "wo":
                    return wo_d[name[1]]
                if name[0] == "wq":
                    return wq_d[name[1], name[2]]
                return pw_d

            def store_gates(L):
                for b in range(TS // TB):
                    n = L * (TS // TB) + b
                    sp.wait_ge(g_out, (n + 1) * (TB // HOT) + 2)
                    sp.dma_start(gates_d[b], gbuf[:, b % 2, :, :]).then_inc(stored[b % 2], 16)

            def expert_loads(L):
                def load_u(q, e, slot):
                    sp.wait_ge(ul_ready, q + 1)
                    sp.dma_start(uraw[:, slot, :], uT_d[L, bass.ds(e, 1)].rearrange("o p n -> (o p) n")).then_inc(uraw_ready[slot], 16)

                def group(g, last=False):
                    for c in range(GROUP):
                        e = g * GROUP + c
                        q = e + L * NKEY
                        sp.wait_ge(vl_ready, q + 1)
                        sp.dma_start(vraw[:, c % 2, :], v_d[L, bass.ds(e * P, P), :] if not last
                                     else v_d[L, e * P:(e + 1) * P, :]).then_inc(vraw_ready[c % 2], 16)
                        if c % 2 == 0:
                            s2 = c // 2
                            sp.wait_ge(wm_ready, q + 2)
                            src = gates_d[:, :, bass.ds(e, 2), :] if not last else gates_d[:, :, e:e + 2, :]
                            sp.dma_start(gp[:, s2, :, :, :].rearrange("p b i t -> p b (i t)"),
                                         src.rearrange("b p i t -> p b (i t)")).then_inc(gp_ready[s2], 16)
                        if not (last and c >= 2):
                            load_u(q + 2, e + 2, c % 2)

                sp.wait_ge(dense_begun, L + 1)
                load_u(L * NKEY, 0, 0)
                load_u(L * NKEY + 1, 1, 1)
                with sp.Fori(0, GROUPS - 1) as g:
                    group(g)
                group(GROUPS - 1, last=True)

            for i in range(2):
                sp.sem_inc(stored[i], 16)
            sp.dma_start(small[:, :], small_d).then_inc(small_ready, 16)
            for n, (name, last) in enumerate(chunks):
                if n >= 2 and name not in (("pool",), ("wq", 1, 0)):
                    u = chunks[n - 2][1]
                    if u in A:
                        sp.wait_ge(a_full, A[u] + 1)
                    else:
                        sp.wait_ge(d_full, Dn[u] + 1)
                src = source(name)
                sp.dma_start(wch[:, n % 2, 0:src.shape[1]], src).then_inc(chunk_ready[n % 2], 16)
                if n == 0:
                    sp.dma_start(const[:, :], const_d).then_inc(in_ready, 16)
                    sp.dma_start(xT[:, :, :], xT_d).then_inc(in_ready, 16)
                    sp.dma_start(trig[:, :, :], trig_d).then_inc(att_in, 16)
                    sp.dma_start(kA[:, :, 0:P], ck_d).then_inc(att_in, 16)
                    sp.dma_start(vA[:, 0, :], cv_d).then_inc(att_in, 16)
                    sp.dma_start(keys[:, :, :], keys_d[0]).then_inc(keys_ready, 16)
                if name == ("wo", 1):
                    sp.wait_ge(rope_done, NH + NKV)
                    sp.dma_start(nk_d, kP[:, :, :]).then_inc(out_done, 16)
                    sp.wait_ge(a_free, A[("v", TILES - 1)] + 1)
                    sp.dma_start(nv_d, vP[:, :]).then_inc(out_done, 16)
                if name == ("wq", 0, 3) or name == ("wq", 1, 3):
                    L = name[1]
                    store_gates(L)
                    expert_loads(L)
                    if L == 0:
                        sp.wait_ge(d_full, Dn[("ob", 0)] + 1)
                        sp.dma_start(keys[:, :, :], keys_d[1]).then_inc(keys_ready, 16)
                        sp.dma_start(inv[:, :, :], inv_d).then_inc(inv_ready, 16)
            for k in range(K):
                sp.wait_ge(y_ready, k + 1)
                sp.dma_start(y_d[:, k, :], hT[:, k, :]).then_inc(out_done, 16)
            sp.wait_ge(out_done, (2 + K) * 16)

        @block.gpsimd
        def _(pool):
            pool.sem_inc(hotg_ready, 1)
            for L in range(DEPTH):
                with pool.Fori(0, PH) as h:
                    pool.wait_ge(mask_ready, h + (L * PH + 1))
                    pool.sem_inc(pool_passed, 1)
                    for c in range(2):
                        last = pool.tensor_tensor(
                            mask[:, c, :, :, :], mask[:, c, :, :, :],
                            topf[:, c, :, :].unsqueeze(2).to_broadcast([P, TILES, TOPK, TOPK]), ALU.mult)
                    last.then_inc(mask_scaled, 1)
                    pool.wait_ge(mask_scaled, h + (L * PH + 1))
                    pool.sem_inc(pool_passed, 1)
                    for c in range(2):
                        last = pool.tensor_tensor(mask[:, c, :, :, 0:TOPK // 2], mask[:, c, :, :, 0:TOPK // 2],
                                                  mask[:, c, :, :, TOPK // 2:TOPK], ALU.add)
                    last.then_inc(mask_done, 1)
                with pool.Fori(1, TILES) as i:
                    pool.wait_ge(pickT_ready, i + L * ST)
                    pool.sem_inc(pool_passed, 1)
                    with pool.Fori(0, P // HOT // SLOTS) as k:
                        for b in range(SLOTS):
                            pool.wait_ge(hot_ready, (i - 1 + L * ST) * (P // HOT) + k * SLOTS + (b + 1))
                            pool.sem_inc(pool_passed, 1)
                            t0 = k * SLOTS * HOT + b * HOT
                            pool.tensor_tensor(
                                hot[:, b, 0, :, :], hot[:, b, 0, :, :],
                                pickT[:, 2, bass.ds(t0, HOT)].unsqueeze(2).to_broadcast([P, HOT, P]),
                                ALU.mult).then_inc(hotg_ready, 1)
                pool.wait_ge(idx_ready, L + 1)
                pool.wait_ge(dense_begun, L + 1)
                for stage, table in enumerate((u_d, v_d)):
                    with pool.Fori(0, ITERS) as i:
                        it = i + (L * 2 + stage) * ITERS
                        for g in range(ROWS // RING):
                            pool.wait_ge(rows_free, it * ROWS + (g * RING + 1))
                            pool.tensor_copy(idxc[:, g, :], idx[:, bass.ds(i * ROWS + g * RING, RING)]
                                             ).then_inc(idx_copied, 1)
                            pool.wait_ge(idx_copied, it * 2 + (g + 1))
                            pool.sem_inc(pool_passed, 1)
                            for j in range(RING):
                                pool.wait_ge(rows_free, it * ROWS + (g * RING + j + 1))
                                pool.sem_inc(pool_passed, 1)
                                pool.indirect_dma_start(
                                    out=rows[:, j, :], out_offset=None, in_=table.rearrange("l e d -> (l e) d"),
                                    in_offset=bass.IndirectOffsetOnAxis(ap=idxc[:, g, j:j + 1], axis=0),
                                ).then_inc(row_ready[j], 16)

        @block.scalar
        def _(act):
            act.wait_ge(small_ready, 16)
            act.activation(cs[:, :, :].rearrange("p k c -> p (k c)"), small[:, O_C:O_C + 2 * K],
                           ACT.Silu).then_inc(cond_ready, 1)
            def scores(L, c):
                n = L * HP + c
                if n >= 2:
                    act.wait_ge(sc_used, n // 2)
                act.wait_ge(sc_full, n + 1)
                act.copy(sc[:, c % 2, :, :], bankD[c % 2][:, 0:T].rearrange("p (t n) -> p t n", n=NKEY)
                         ).then_inc(sc_copied, 1)

            def route_copies(L):
                act.wait_ge(gexp_in, L + 1)
                act.activation(gt[:, :, :], gt[:, :, :], ACT.Exp).then_inc(gexp_out, 1)
                act.copy(hh[:, :, :], hT[:, :, 0:TS]).then_inc(split_h, 1)
                for i in range(1, TILES):
                    for half in range(2):
                        n0 = ((L * ST + i - 1) * 2 + half) * (TB // HOT)
                        act.wait_ge(stored[half], 16 * (L * ST + i))
                        with act.Fori(0, TB // HOT // 2) as k:
                            for b in range(2):
                                act.wait_ge(g_full, k * 2 + (n0 + b + 1 + SLOTS))
                                act.copy(gbuf[:, half, :, bass.ds(k * 2 * HOT + b * HOT, HOT)],
                                         bankD[1][:, b * 512:(b + 1) * 512].rearrange("p (t i) -> p i t", i=NKEY)
                                         ).then_inc(g_out, 1)

            def experts(L):
                def split_u(q, b):
                    act.wait_ge(a_done, q + 1)
                    act.sem_inc(act_passed, 1)
                    act.wait_ge(uraw_ready[b], q * 8 + (16 - 8 * b))
                    act.copy(uh[:, b, :], uraw[:, b, :]).then_inc(uh_ready, 1)

                def group(g, last=False):
                    for c in range(GROUP):
                        q = g * GROUP + (c + L * NKEY)
                        act.wait_ge(out_full, g * K + (L * GROUPS * K + 1))
                        act.sem_inc(act_passed, 1)
                        act.wait_ge(vraw_ready[c % 2], q * 8 + (16 - 8 * (c % 2)))
                        act.copy(vh[:, c, :], vraw[:, c % 2, :]).then_inc(vh_ready, 1)
                        act.wait_ge(wl_ready, q + 1)
                        act.sem_inc(act_passed, 1)
                        act.wait_ge(a_done, q + 3)
                        act.activation(wt[:, c % 2, :], abank[c % 2], ACT.Gelu).then_inc(gelu_ready, 1)
                        act.wait_ge(wm_ready, q + 5)
                        act.copy(wh[:, c, :], wt[:, c % 2, :]).then_inc(wh_ready, 1)
                        if not (last and c >= 2):
                            split_u(q + 2, c % 2)

                split_u(L * NKEY, 0)
                split_u(L * NKEY + 1, 1)
                with act.Fori(0, ITERS) as g:
                    group(g)
                act.wait_ge(u_done, L + 1)
                act.activation(actg[:, :], aval[:, :], ACT.Gelu).then_inc(gelu_done, 1)
                with act.Fori(ITERS, GROUPS - 1) as g:
                    group(g)
                group(GROUPS - 1, last=True)

            act.sem_inc(gelu_ready, 2)
            act.sem_inc(g_out, 2)
            for name, cls in ORDER:
                if cls != "A":
                    continue
                n = A[name]
                bank = bankA[n % 2]
                kind = name[0]
                if kind == "norm":
                    i = name[1]
                    if i == 0:
                        act.wait_ge(in_ready, 32)
                        act.wait_ge(step, 1)
                    for k in range(K):
                        if i in (1, 3):
                            act.wait_ge(d_free, Dn[("wo", k) if i == 1 else ("pool", k | 1)] + 1)
                        elif i:
                            act.wait_ge(x_ready, (i // 2 - 1) * K + k + 1)
                        act.activation(sq[:, k, :], xT[:, k, :], ACT.Square).then_inc(sq_ready, 1)
                    act.wait_ge(a_full, n + 1)
                    act.activation(std[:, :], bank[:, 0:T], ACT.Sqrt, bias=epsb[:, 0:1],
                                   scale=1.0 / D).then_inc(a_free, 1)
                    if i < 4:
                        L, half = divmod(i, 2)
                        for k in range(K):
                            act.wait_ge(scaled, i * K + k + 1)
                            for c, (a, b) in enumerate(SEGS):
                                last = act.activation(hT[:, k, a:b], hT[:, k, a:b], ACT.Identity,
                                                      bias=mod[:, L, 3 * half, k, c:c + 1])
                            last.then_inc(h_ready, 1)
                    continue
                if kind in ("proj", "hsum") and name[1] >= 2:
                    act.wait_ge(qn_ready, name[1] - 1)
                if kind == "score":
                    act.wait_ge(negmax_ready, name[1] + 1)
                    if name[1] >= 2:
                        act.wait_ge(d_full, Dn[("pt", name[1] - 2)] + 1)
                if kind == "htok":
                    scores(name[1], HP - 1)
                    route_copies(name[1])
                    act.wait_ge(dense_begun, name[1] + 1)
                act.wait_ge(a_full, n + 1)
                if kind == "ada":
                    act.copy(adar[:, name[2] % 2, :], bank[0:2, 0:CH]).then_inc(a_free, 1)
                elif kind == "adat":
                    L, j = name[1:]
                    act.copy(mod[:, L, j // 2, 4 * (j % 2):4 * (j % 2) + 4, :],
                             bank[:, 0:8].rearrange("p (m c) -> p m c", c=2)).then_inc(a_free, 1)
                elif kind == "proj":
                    b = name[1] % 2
                    act.activation(hsq[:, b, :], bank[:, 0:T], ACT.Square).then_inc(hsq_ready, 1)
                    act.copy(qraw[:, b, :], bank[:, 0:T]).then_inc(a_free, 1)
                elif kind == "hsum":
                    act.activation(hstd[:, name[1] % 2, :], bank[:, 0:T], ACT.Sqrt, bias=epsb[:, 0:1],
                                   scale=1.0 / HD).then_inc(a_free, 1)
                elif kind == "v":
                    dst = vA[:, 1 + name[1], :] if name[1] < TILES - 1 else vP[:, :]
                    act.copy(dst, bank[:, 0:NKV * HD]).then_inc(a_free, 1)
                elif kind == "score":
                    b = name[1] % 2
                    w = KT * P if name[1] % TILES < TILES - 1 else P
                    act.activation(prob[:, b, 0:w], bank[:, 0:w], ACT.Exp, bias=smx[:, b, 1:2],
                                   scale=SCALE, accum_out=smx[:, b, 2:3]).then_inc(a_free, 1)
                elif kind == "pv":
                    act.copy(OT[:, name[1], :], bank[:, 0:T]).then_inc(a_free, 1)
                elif kind == "wq":
                    act.copy(qT[:, name[2], :], bank[:, 0:T]).then_inc(a_free, 1)
                    if name[2]:
                        scores(name[1], name[2] - 1)
                elif kind == "htok":
                    act.copy(htok[:, :], bank[:, :]).then_inc(a_free, 1)
                    experts(name[1])

        @block.vector
        def _(v):
            steps = [0]

            def then(ins):
                steps[0] += 1
                ins.then_inc(step, 1)
                v.wait_ge(step, steps[0])

            def modulation(L, j0, j1, norms):
                bias = small[:, O_B + L * 6 * K:O_B + (L + 1) * 6 * K].rearrange("p (j k) -> p j k", j=6)
                v.wait_ge(a_free, A[("adat", L, j1 * D // CH - 1)] + 1)
                then(v.tensor_tensor(mod[:, L, j0:j1, :, :], mod[:, L, j0:j1, :, :],
                                     bias[:, j0:j1].unsqueeze(3).to_broadcast([P, j1 - j0, K, 2]), ALU.add))
                for n in norms:
                    g0 = O_G + (2 * L + n) * K
                    then(v.scalar_tensor_tensor(out=amod[:, L, n, :, :], in0=mod[:, L, 3 * n + 1, :, :], scalar=1.0,
                                                in1=small[:, g0:g0 + K].unsqueeze(2).to_broadcast([P, K, 2]),
                                                op0=ALU.add, op1=ALU.mult))
                if L == 1:
                    then(v.tensor_tensor(mod[:, L, 2, :, :], mod[:, L, 2, :, :],
                                         small[:, O_PS:O_PS + K].unsqueeze(2).to_broadcast([P, K, 2]), ALU.mult))

            def norm(i):
                L, n = divmod(i, 2)
                v.wait_ge(a_free, A[("norm", i)] + 1)
                then(v.reciprocal(std[:, :], std[:, :]))
                for k in range(K):
                    for c, (a, b) in enumerate(((0, T),) if i == 4 else SEGS):
                        gain = small[:, O_G + 4 * K + k:O_G + 4 * K + k + 1] if i == 4 else amod[:, L, n, k, c:c + 1]
                        last = v.scalar_tensor_tensor(out=hT[:, k, a:b], in0=xT[:, k, a:b], scalar=gain,
                                                      in1=std[:, a:b], op0=ALU.mult, op1=ALU.mult)
                    last.then_inc(y_ready if i == 4 else scaled, 1)

            def update(name, m, gate_of, ra=0, segs=SEGS):
                n = Dn[name]
                v.wait_ge(d_full, n + 1)
                for a, b in segs:
                    c = 0 if a < TS else 1
                    last = v.scalar_tensor_tensor(out=xT[:, m, a:b], in0=bankD[n % 2][:, a:b],
                                                  scalar=mod[:, gate_of[0], gate_of[1], m, c:c + 1],
                                                  in1=xT[:, m, a:b], op0=ALU.mult, op1=ALU.add)
                last.then_inc(d_free, 1)

            def attention():
                v.wait_ge(att_in, 48)

                def head_norm(s):
                    b = s % 2
                    v.wait_ge(a_free, A[("hsum", s)] + 1)
                    then(v.reciprocal(hstd[:, b, :], hstd[:, b, :]))
                    g = small[:, O_H + (s >= NH):O_H + (s >= NH) + 1]
                    dst = QT[:, s, TS:T] if s < NH else kP[:, s - NH, :]
                    v.scalar_tensor_tensor(out=dst, in0=qraw[:, b, TS:T], scalar=g, in1=hstd[:, b, TS:T],
                                           op0=ALU.mult, op1=ALU.mult)
                    v.scalar_tensor_tensor(out=qn[:, b, :], in0=qraw[:, b, 0:TS], scalar=g, in1=hstd[:, b, 0:TS],
                                           op0=ALU.mult, op1=ALU.mult).then_inc(qn_ready, 1)

                def rotary(s):
                    n = Dn[("rot", s)]
                    v.wait_ge(qn_ready, s + 1)
                    if s:
                        v.wait_ge(rope_done, s)
                    v.tensor_tensor(ropes[:, 0, :], qn[:, s % 2, :], trig[:, 0, :], ALU.mult)
                    v.wait_ge(d_full, n + 1)
                    v.tensor_tensor(ropes[:, 1, :], bankD[n % 2][:, 0:TS], trig[:, 1, :], ALU.mult).then_inc(d_free, 1)
                    v.wait_ge(d_free, n + 1)
                    dst = QT[:, s, 0:TS] if s < NH else kA[:, s - NH, P:KT * P]
                    v.tensor_tensor(dst, ropes[:, 0, :], ropes[:, 1, :], ALU.add).then_inc(rope_done, 1)

                for s in range(NH + NKV + 1):
                    if s < NH + NKV:
                        head_norm(s)
                    if s >= 1:
                        rotary(s - 1)

                def row_max(n):
                    w = KT * P if n % TILES < TILES - 1 else P
                    u = A[("score", n)]
                    if n >= 2:
                        v.wait_ge(prob_ready, n - 1)
                    v.wait_ge(a_full, u + 1)
                    then(v.tensor_reduce(smx[:, n % 2, 0:1], bankA[u % 2][:, 0:w], AX.X, ALU.max))
                    v.tensor_scalar(smx[:, n % 2, 1:2], smx[:, n % 2, 0:1], -SCALE, None, ALU.mult
                                    ).then_inc(negmax_ready, 1)

                def normalise(n):
                    w = KT * P if n % TILES < TILES - 1 else P
                    v.wait_ge(a_free, A[("score", n)] + 1)
                    then(v.reciprocal(smx[:, n % 2, 3:4], smx[:, n % 2, 2:3]))
                    v.tensor_scalar(prob[:, n % 2, 0:w], prob[:, n % 2, 0:w], smx[:, n % 2, 3:4], None, ALU.mult
                                    ).then_inc(prob_ready, 1)

                def keep_transposed(n):
                    h, t = divmod(n, TILES)
                    u = Dn[("pt", n)]
                    if t == 0 and h >= 2:
                        v.wait_ge(a_full, A[("pv", h - 2)] + 1)
                    v.wait_ge(d_full, u + 1)
                    if t < TILES - 1:
                        v.tensor_copy(PT[:, h % 2, :, t * P:(t + 1) * P],
                                      bankD[u % 2][:, 0:KT * P].rearrange("p (j q) -> p j q", q=P)).then_inc(d_free, 1)
                    else:
                        v.tensor_copy(PTp[:, h % 2, :], bankD[u % 2][:, 0:P]).then_inc(d_free, 1)

                for n in range(NH * TILES + 2):
                    if n < NH * TILES:
                        row_max(n)
                    if 1 <= n <= NH * TILES:
                        normalise(n - 1)
                    if n >= 2:
                        keep_transposed(n - 2)
                modulation(0, 2, 6, (1,))
                for m in range(K):
                    update(("wo", m), m, (0, 2))

            def pooling():
                v.wait_ge(inv_ready, 16)
                v.wait_ge(h_ready, 3 * K)
                then(v.memset(pad[:, :, :, :], 0.0))
                for j, win in enumerate(WINDOWS):
                    h2 = hT[:, 2 * j:2 * j + 2, :]
                    for c, (a, b) in enumerate(SEGS):
                        last = v.tensor_copy(pad[:, 0, :, PSEG[c][0]:PSEG[c][1]], h2[:, :, a:b])
                    then(last)
                    s, w, src = 1, PW, 0
                    while s < win:
                        w -= s
                        dst = 1 if src != 1 else 2
                        then(v.tensor_tensor(pad[:, dst, :, 0:w], pad[:, src, :, 0:w], pad[:, src, :, s:s + w], ALU.add))
                        s, src = 2 * s, dst
                    for c, (a, b) in enumerate(SEGS):
                        p0 = PSEG[c][0] - win // 2
                        last = v.tensor_tensor(sq[:, 2 * j:2 * j + 2, a:b], pad[:, src, :, p0:p0 + b - a],
                                               inv[:, j, a:b].unsqueeze(1).to_broadcast([P, 2, b - a]), ALU.mult)
                    then(last)
                    v.tensor_tensor(sq[:, 2 * j:2 * j + 2, :], sq[:, 2 * j:2 * j + 2, :], h2, ALU.subtract
                                    ).then_inc(pooled_ready, 1)
                for m in range(K):
                    update(("pool", m), m, (1, 2))

            def routing(L):
                base = steps[0]
                per_head = 9
                if L == 0:
                    v.wait_ge(out_done, 32)

                def key_numbers(h):
                    v.wait_ge(mask_done, h + (L * PH + 1))
                    v.sem_inc(dve_passed, 1)
                    for c in range(2):
                        last = v.tensor_reduce(i12[:, :, c, bass.ds(h * TOPK, TOPK) if not isinstance(h, int)
                                                   else slice(h * TOPK, (h + 1) * TOPK)],
                                               mask[:, c, :, :, 0:TOPK // 2], AX.X, ALU.add)
                    return last

                def head(h, first=False):
                    done = [0]

                    def then_h(ins):
                        done[0] += 1
                        ins.then_inc(step, 1)
                        v.wait_ge(step, h * per_head + (base + done[0]))
                        v.sem_inc(dve_passed, 1)

                    sets = [(c, t) for c in range(2) for t in range(TILES)]
                    v.wait_ge(sc_copied, h * 2 + (L * HP + 2))
                    v.sem_inc(dve_passed, 1)
                    for c, t in sets:
                        last = v.max(top[:, c, t, 0:8], sc[:, c, t, :])
                    then_h(last)
                    for c, t in sets:
                        v.max_index(topi[:, c, t, 0:8], top[:, c, t, 0:8], sc[:, c, t, :])
                    for c, t in sets:
                        last = v.match_replace(out=sc2[:, c, t, :], in_to_replace=top[:, c, t, 0:8],
                                               in_values=sc[:, c, t, :], imm_value=LOWEST)
                    last.then_inc(sc_used, 1)
                    v.wait_ge(sc_used, h + (L * PH + 1))
                    v.sem_inc(dve_passed, 1)
                    for c, t in sets:
                        last = v.max(top[:, c, t, 8:16], sc2[:, c, t, :])
                    then_h(last)
                    for c, t in sets:
                        last = v.max_index(topi[:, c, t, 8:16], top[:, c, t, 8:16], sc2[:, c, t, :])
                    last = v.tensor_tensor(cand[:, :, :].rearrange("p t (a b) -> p t a b", b=TOPK),
                                           top[:, 0, :, :].unsqueeze(3).to_broadcast([P, TILES, TOPK, TOPK]),
                                           top[:, 1, :, :].unsqueeze(2).to_broadcast([P, TILES, TOPK, TOPK]), ALU.add)
                    if not first:
                        last = key_numbers(h - 1)
                    then_h(last)
                    v.tensor_copy(topf[:, :, :, :], topi[:, :, :, :])
                    for t in range(TILES):
                        last = v.max(csv[:, t, 0:8], cand[:, t, :])
                    then_h(last)
                    for t in range(TILES):
                        v.max_index(csi[:, t, 0:8], csv[:, t, 0:8], cand[:, t, :])
                    for t in range(TILES):
                        last = v.match_replace(out=cand2[:, t, :], in_to_replace=csv[:, t, 0:8],
                                               in_values=cand[:, t, :], imm_value=LOWEST)
                    then_h(last)
                    for t in range(TILES):
                        last = v.max(csv[:, t, 8:16], cand2[:, t, :])
                    then_h(last)
                    for t in range(TILES):
                        last = v.max_index(csi[:, t, 8:16], csv[:, t, 8:16], cand2[:, t, :])
                    then_h(last)
                    v.tensor_copy(gt[:, :, 0:TOPK] if first else gt[:, :, bass.ds(h * TOPK, TOPK)], csv[:, :, :])
                    ci = csi[:, :, :].rearrange("p t k -> p (t k)")
                    v.tensor_scalar(pick[:, 0, :], ci, 4, None, ALU.logical_shift_right)
                    then_h(v.tensor_scalar(pick[:, 1, :], ci, TOPK - 1, None, ALU.bitwise_and))
                    then_h(v.tensor_copy(pickf[:, :, :], pick[:, :, :]))
                    n = TILES * TOPK
                    for c in range(2):
                        last = v.tensor_tensor(mask[:, c, :, :, :].rearrange("p t k a -> p (t k) a"),
                                               pickf[:, c, :].unsqueeze(2).to_broadcast([P, n, TOPK]),
                                               iota[:, 0:TOPK].unsqueeze(1).to_broadcast([P, n, TOPK]), ALU.is_equal)
                    last.then_inc(mask_ready, 1)
                    v.wait_ge(mask_ready, h + (L * PH + 1))
                    v.sem_inc(dve_passed, 1)
                    assert done[0] == per_head, done[0]

                head(0, first=True)
                with v.Fori(1, PH) as h:
                    head(h)
                steps[0] += per_head * PH
                then(key_numbers(PH - 1))

                g3 = gt[:, :, :].rearrange("p t (h k) -> p (t h) k", k=TOPK)
                then(v.tensor_copy(gsum[:, :], g3[:, :, 0]))
                v.tensor_tensor(g3, g3, gsum[:, :].unsqueeze(2).to_broadcast([P, TILES * PH, TOPK]), ALU.subtract
                                ).then_inc(gexp_in, 1)
                v.wait_ge(gexp_out, L + 1)
                then(v.tensor_reduce(gsum[:, :], g3, AX.X, ALU.add))
                then(v.reciprocal(gsum[:, :], gsum[:, :]))
                v.tensor_tensor(g3, g3, gsum[:, :].unsqueeze(2).to_broadcast([P, TILES * PH, TOPK]), ALU.mult
                                ).then_inc(routed, 1)
                v.wait_ge(routed, L + 1)
                v.tensor_copy(gate[:, :], gt[:, TILES - 1, :])
                i1, i2 = i12[:, TILES - 1, 0, :], i12[:, TILES - 1, 1, :]
                then(v.tensor_scalar(i1, i1, float(L * NKEY), None, ALU.add))
                v.scalar_tensor_tensor(out=idx[:, :], in0=i1, scalar=float(NKEY), in1=i2,
                                       op0=ALU.mult, op1=ALU.add).then_inc(idx_ready, 1)

                with v.Fori(1, TILES) as i:
                    v.wait_ge(pickT_full, i + L * ST)
                    v.sem_inc(dve_passed, 1)
                    v.wait_ge(hotg_ready, (i - 1 + L * ST) * (P // HOT) + 1)
                    v.tensor_copy(pickT[:, :, :], bankD[0][:, 0:3 * P].rearrange("p (j t) -> p j t", j=3)
                                  ).then_inc(pickT_ready, 1)
                    v.wait_ge(pickT_ready, i + L * ST)
                    v.sem_inc(dve_passed, 1)
                    with v.Fori(0, P // HOT // SLOTS) as k:
                        for b in range(SLOTS):
                            n = (i - 1 + L * ST) * (P // HOT) + k * SLOTS + b
                            t0 = k * SLOTS * HOT + b * HOT
                            v.wait_ge(g_full, n + 1)
                            v.sem_inc(dve_passed, 1)
                            v.tensor_tensor(
                                hot[:, b, :, :, :],
                                pickT[:, 0:2, bass.ds(t0, HOT)].unsqueeze(3).to_broadcast([P, 2, HOT, P]),
                                iota.unsqueeze(1).unsqueeze(1).to_broadcast([P, 2, HOT, P]), ALU.is_equal
                            ).then_inc(hot_ready, 1)
                    v.wait_ge(hot_ready, (i + L * ST) * (P // HOT))
                    v.sem_inc(dve_passed, 1)

            def experts(L):
                def split_u(q, b):
                    v.wait_ge(uh_ready, q + 1)
                    v.tensor_tensor(ul[:, b, :], uraw[:, b, :], uh[:, b, :].bitcast(F32), ALU.subtract
                                    ).then_inc(ul_ready, 1)

                def u_row(g, r):
                    n = (g + L * 2 * ITERS) * (ROWS // RING) + r // RING
                    v.wait_ge(row_ready[r % RING], n * 16 + 16)
                    v.tensor_tensor_reduce(out=rows[:, r % RING, :], in0=rows[:, r % RING, :], in1=htok[:, :],
                                           scale=1.0, scalar=0.0, op0=ALU.mult, op1=ALU.add,
                                           accum_out=a8[:, r:r + 1]).then_inc(rows_free, 1)

                def v_row(g, r):
                    it = g - ITERS + (L * 2 + 1) * ITERS
                    v.wait_ge(row_ready[r % RING], (it * (ROWS // RING) + r // RING) * 16 + 16)
                    v.wait_ge(rows_free, it * ROWS + (RING + r - 1))
                    v.scalar_tensor_tensor(out=acc[:, r % 2, :], in0=rows[:, r % RING, :], scalar=a8[:, r:r + 1],
                                           in1=acc[:, r % 2, :], op0=ALU.mult, op1=ALU.add).then_inc(rows_free, 1)

                def group(g, row, last=False):
                    for c in range(GROUP):
                        q = g * GROUP + (c + L * NKEY)
                        v.wait_ge(gelu_ready, q + 3)
                        v.wait_ge(gp_ready[c // 2], (g + L * GROUPS) * 16 + 16)
                        w3 = wt[:, c % 2, :].rearrange("p (b t) -> p b t", t=TB)
                        v.tensor_tensor(w3, w3, gp[:, c // 2, :, c % 2, :], ALU.mult).then_inc(wm_ready, 1)
                        v.wait_ge(vh_ready, q + 1)
                        v.tensor_tensor(vl[:, c, :], vraw[:, c % 2, :], vh[:, c, :].bitcast(F32), ALU.subtract
                                        ).then_inc(vl_ready, 1)
                        v.wait_ge(wh_ready, q + 1)
                        v.tensor_tensor(wl[:, c, :], wt[:, c % 2, :], wh[:, c, :].bitcast(F32), ALU.subtract
                                        ).then_inc(wl_ready, 1)
                        if not (last and c >= 2):
                            split_u(q + 2, c % 2)
                    for m in range(K):
                        row(g, m)
                        r = g * K + (m + L * GROUPS * K)
                        v.wait_ge(acc_done, r + 1)
                        v.wait_ge(out_full, r + 2)
                        v.tensor_tensor(hT[:, m, 0:TS], obank[m % 4], hT[:, m, 0:TS], ALU.add).then_inc(acc_done, 1)

                v.wait_ge(split_h, L + 1)
                v.tensor_tensor(hl[:, :, :], hT[:, :, 0:TS], hh[:, :, :].bitcast(F32), ALU.subtract).then_inc(h_split, 1)
                v.wait_ge(h_split, L + 1)
                v.memset(hT[:, :, 0:TS], 0.0)
                v.wait_ge(g_out, (L + 1) * ST * (P // HOT) + 2)
                for i in range(2):
                    v.wait_ge(stored[i], 16 * ((L + 1) * ST + 1))
                v.sem_inc(dense_begun, 1)
                then(v.memset(acc[:, :, :], 0.0))
                v.wait_ge(a_free, A[("htok", L)] + 1)
                split_u(L * NKEY, 0)
                split_u(L * NKEY + 1, 1)
                with v.Fori(0, ITERS) as g:
                    group(g, u_row)
                    v.wait_ge(rows_free, g * ROWS + (L * 2 * ITERS * ROWS + ROWS + RING))
                    v.tensor_copy(aval[:, bass.ds(g * ROWS, ROWS)], a8[:, :]).then_inc(step, 1)
                    v.wait_ge(step, g + (steps[0] + 1))
                    v.sem_inc(dve_passed, 1)
                steps[0] += ITERS
                v.sem_inc(u_done, 1)
                v.wait_ge(gelu_done, L + 1)
                then(v.tensor_tensor(actg[:, :], actg[:, :], gate[:, :], ALU.mult))

                def v_group(g, last=False):
                    it = g - ITERS + (L * 2 + 1) * ITERS
                    v.wait_ge(rows_free, it * ROWS + RING)
                    i0 = (g - ITERS) * ROWS
                    v.tensor_copy(a8[:, :], actg[:, i0:i0 + ROWS] if last else actg[:, bass.ds(i0, ROWS)]
                                  ).then_inc(step, 1)
                    v.wait_ge(step, g - ITERS + (steps[0] + 1))
                    v.sem_inc(dve_passed, 1)
                    group(g, v_row, last)

                with v.Fori(ITERS, GROUPS - 1) as g:
                    v_group(g)
                v_group(GROUPS - 1, last=True)
                steps[0] += ITERS
                v.wait_ge(rows_free, RING + (L + 1) * 2 * P)
                v.tensor_tensor(acc[:, 0, :], acc[:, 0, :], acc[:, 1, :], ALU.add).then_inc(acc_ready, 1)
                v.wait_ge(acc_done, (L + 1) * GROUPS * K + K)
                n = Dn[("ob", L)]
                v.wait_ge(d_full, n + 1)
                for m in range(K):
                    last = v.scalar_tensor_tensor(out=xT[:, m, TS:T], in0=bankD[n % 2][:, m * P:(m + 1) * P],
                                                  scalar=mod[:, L, 5, m, 1:2], in1=xT[:, m, TS:T],
                                                  op0=ALU.mult, op1=ALU.add)
                    if m == K - 1:
                        last.then_inc(d_free, 1)
                    v.scalar_tensor_tensor(out=xT[:, m, 0:TS], in0=hT[:, m, 0:TS], scalar=mod[:, L, 5, m, 0:1],
                                           in1=xT[:, m, 0:TS], op0=ALU.mult, op1=ALU.add).then_inc(x_ready, 1)
                v.wait_ge(x_ready, (L + 1) * K)

            then(v.memset(epsb[:, :], EPS))
            v.sem_inc(rows_free, RING)
            v.sem_inc(ul_ready, 2)
            v.sem_inc(vl_ready, 2)
            v.sem_inc(wl_ready, 2)
            v.sem_inc(wm_ready, 4)
            v.sem_inc(acc_done, K)
            v.wait_ge(small_ready, 16)
            v.wait_ge(in_ready, 32)
            modulation(0, 0, 2, (0,))
            norm(0)
            attention()
            modulation(1, 0, 6, (0, 1))
            norm(1)
            routing(0)
            experts(0)
            norm(2)
            pooling()
            norm(3)
            routing(1)
            experts(1)
            norm(4)

        @block.tensor
        def _(pe):
            def chunk(name, cols=CH):
                n = CN[name]
                pe.wait_ge(chunk_ready[n % 2], 16 * (n // 2 + 1))
                return wch[:, n % 2, :].rearrange("p (k n) -> p k n", n=cols)

            def scores(L, c):
                if c == 0:
                    pe.wait_ge(d_free, Dn[("wo", K - 1) if L == 0 else ("pool", K - 1)] + 1)
                    pe.wait_ge(keys_ready, 16 * (L + 1))
                n = L * HP + c
                if n >= 2:
                    pe.wait_ge(sc_copied, n - 1)
                pe.wait_ge(a_free, A[("wq", L, c)] + 1)
                for t in range(TILES):
                    last = pe.matmul(bankD[c % 2][:, t * P:(t + 1) * P], qT[:, c, t * P:(t + 1) * P], keys[:, c, :],
                                     start=True, stop=True)
                last.then_inc(sc_full, 1)

            def gates(L):
                pe.wait_ge(routed, L + 1)
                pe.wait_ge(sc_copied, HP * (L + 1))
                for i in range(1, TILES):
                    t = TILE_ORDER[i]
                    if L * ST + i > 1:
                        pe.wait_ge(pickT_ready, L * ST + i - 1)
                    pe.transpose(bankD[0][:, 0:P], i12[:, t, 0, :], ident)
                    pe.transpose(bankD[0][:, P:2 * P], i12[:, t, 1, :], ident)
                    pe.transpose(bankD[0][:, 2 * P:3 * P], gt[:, t, :], ident).then_inc(pickT_full, 1)
                    with pe.Fori(0, P // HOT // SLOTS) as k:
                        for b in range(SLOTS):
                            n = k * SLOTS + ((L * ST + i - 1) * (P // HOT) + b)
                            pe.wait_ge(g_out, n + 1)
                            pe.wait_ge(hotg_ready, n + 2)
                            o = b % 2 * 512
                            for j in range(HOT):
                                last = pe.matmul(bankD[1][:, o + j * P:o + (j + 1) * P],
                                                 hot[:, b, 1, j, :], hot[:, b, 0, j, :], start=True, stop=True)
                            last.then_inc(g_full, 1)
                pe.wait_ge(g_out, (L + 1) * ST * (P // HOT) + 2)

            def experts(L):
                def group(g):
                    for c in range(GROUP):
                        q = g * GROUP + (c + L * NKEY)
                        pe.wait_ge(gelu_ready, q + 1)
                        pe.wait_ge(ul_ready, q + 3)
                        bank = abank[c % 2]
                        for k in range(K):
                            hi, lo = uh[:, c % 2, k * P:(k + 1) * P], ul[:, c % 2, k * P:(k + 1) * P]
                            pe.matmul(bank, hi, hh[:, k, :], start=k == 0, stop=False)
                            pe.matmul(bank, hi, hl[:, k, :], start=False, stop=False)
                            last = pe.matmul(bank, lo, hh[:, k, :], start=False, stop=k == K - 1)
                        last.then_inc(a_done, 1)

                    def out(m, chunks):
                        for c in chunks:
                            hi, lo = vh[:, c, m * P:(m + 1) * P], vl[:, c, m * P:(m + 1) * P]
                            pe.matmul(obank[m % 4], hi, wh[:, c, :], start=c == 0, stop=False)
                            pe.matmul(obank[m % 4], hi, wl[:, c, :], start=False, stop=False)
                            last = pe.matmul(obank[m % 4], lo, wh[:, c, :], start=False, stop=c == GROUP - 1)
                        return last

                    q = g * GROUP + L * NKEY
                    r = g * K + L * GROUPS * K
                    pe.wait_ge(wl_ready, q + (GROUP - 1 + 2))
                    pe.wait_ge(vl_ready, q + (GROUP - 1 + 2))
                    for m in range(2):
                        pe.wait_ge(acc_done, r + (m + 1 + K - 4))
                        out(m, range(GROUP - 1))
                    pe.wait_ge(wl_ready, q + (GROUP + 2))
                    pe.wait_ge(vl_ready, q + (GROUP + 2))
                    for m in range(2):
                        out(m, (GROUP - 1,)).then_inc(out_full, 1)
                    for m in range(2, K):
                        pe.wait_ge(acc_done, r + (m + 1 + K - 4))
                        last = out(m, range(GROUP))
                        if m < K - 1:
                            last.then_inc(out_full, 1)
                    last.then_inc(out_full, 1)

                pe.wait_ge(h_split, L + 1)
                pe.wait_ge(split_h, L + 1)
                with pe.Fori(0, GROUPS) as g:
                    group(g)
                pe.wait_ge(acc_done, (L + 1) * GROUPS * K + K)

            pe.sem_inc(g_full, SLOTS)
            pe.sem_inc(a_done, 2)
            pe.sem_inc(out_full, 1)
            for name, cls in ORDER:
                kind = name[0]
                n = (A if cls == "A" else Dn)[name]
                bank = (bankA if cls == "A" else bankD)[n % 2]
                full = a_full if cls == "A" else d_full
                if kind == "htok":
                    scores(name[1], HP - 1)
                    gates(name[1])
                if kind == "ob":
                    experts(name[1])
                if n >= 2:
                    pe.wait_ge(a_free if cls == "A" else d_free, n - 1)
                if kind == "ada":
                    L, j = name[1:]
                    if j == 0 and L == 0:
                        pe.wait_ge(cond_ready, 1)
                    w = chunk(name)
                    for k in range(K):
                        last = pe.matmul(bank[0:2, 0:CH], cs[:, k, :], w[:, k, :], start=k == 0, stop=k == K - 1)
                elif kind == "adat":
                    pe.wait_ge(a_free, A[("ada",) + name[1:]] + 1)
                    pe.wait_ge(in_ready, 32)
                    for m in range(CH // P):
                        last = pe.transpose(bank[:, 2 * m:2 * m + 2], adar[:, name[2] % 2, m * P:(m + 1) * P],
                                            ident[0:2, 0:2])
                elif kind == "norm":
                    pe.wait_ge(in_ready, 32)
                    for k in range(K):
                        pe.wait_ge(sq_ready, name[1] * K + k + 1)
                        for a, b in SEGS:
                            last = pe.matmul(bank[:, a:b], ones, sq[:, k, a:b], start=k == 0, stop=k == K - 1)
                elif kind in ("proj", "wq"):
                    c = name[-1]
                    w = chunk(("qkv", c // 4) if kind == "proj" else ("wq", name[1], c // 4))
                    for k in range(K):
                        if c == 0:
                            pe.wait_ge(h_ready, (0 if kind == "proj" else 1 + 2 * name[1]) * K + k + 1)
                        for a, b in SEGS:
                            last = pe.matmul(bank[:, a:b], w[:, k, (c % 4) * P:(c % 4 + 1) * P], hT[:, k, a:b],
                                             start=k == 0, stop=k == K - 1)
                elif kind == "hsum":
                    pe.wait_ge(hsq_ready, name[1] + 1)
                    for a, b in SEGS:
                        last = pe.matmul(bank[:, a:b], ones, hsq[:, name[1] % 2, a:b], start=True, stop=True)
                elif kind == "rot":
                    pe.wait_ge(qn_ready, name[1] + 1)
                    last = pe.matmul(bank[:, 0:TS], rotp, qn[:, name[1] % 2, :], start=True, stop=True)
                elif kind == "v":
                    t = name[1]
                    w = chunk(("qkv", 2))
                    for k in range(K):
                        last = pe.matmul(bank[:, 0:NKV * HD], hT[:, k, t * P:(t + 1) * P], w[:, k, NKV * HD:CH],
                                         start=k == 0, stop=k == K - 1)
                elif kind == "score":
                    h, t = divmod(name[1], TILES)
                    if name[1] == 0:
                        pe.wait_ge(rope_done, NH + NKV)
                        pe.wait_ge(att_in, 48)
                    kv = h // (NH // NKV)
                    q = QT[:, h, t * P:(t + 1) * P]
                    if t < TILES - 1:
                        pe.matmul(bank[:, 0:512], q, kA[:, kv, 0:512], start=True, stop=True)
                        last = pe.matmul(bank[:, 512:KT * P], q, kA[:, kv, 512:KT * P], start=True, stop=True)
                    else:
                        last = pe.matmul(bank[:, 0:P], q, kP[:, kv, :], start=True, stop=True)
                elif kind == "pt":
                    pe.wait_ge(prob_ready, name[1] + 1)
                    for j in range(KT if name[1] % TILES < TILES - 1 else 1):
                        last = pe.transpose(bank[:, j * P:(j + 1) * P], prob[:, name[1] % 2, j * P:(j + 1) * P], ident)
                elif kind == "pv":
                    h = name[1]
                    kv = h // (NH // NKV)
                    pe.wait_ge(d_free, Dn[("pt", h * TILES + TILES - 1)] + 1)
                    pe.wait_ge(a_free, A[("v", TILES - 1)] + 1)
                    for j in range(KT):
                        pe.matmul(bank[:, 0:TS], vA[:, j, kv * HD:(kv + 1) * HD], PT[:, h % 2, j, :],
                                  start=j == 0, stop=j == KT - 1)
                    last = pe.matmul(bank[:, TS:T], vP[:, kv * HD:(kv + 1) * HD], PTp[:, h % 2, :], start=True, stop=True)
                elif kind == "wo":
                    m = name[1]
                    pe.wait_ge(a_free, A[("pv", NH - 1)] + 1)
                    w = chunk(("wo", m // 4))
                    for h in range(NH):
                        for a, b in SEGS:
                            last = pe.matmul(bank[:, a:b], w[:, h, (m % 4) * P:(m % 4 + 1) * P], OT[:, h, a:b],
                                             start=h == 0, stop=h == NH - 1)
                elif kind == "htok":
                    for m in range(K):
                        last = pe.transpose(bank[:, m * P:(m + 1) * P], hT[:, m, TS:T], ident)
                elif kind == "ob":
                    pe.wait_ge(acc_ready, name[1] + 1)
                    for m in range(K):
                        last = pe.transpose(bank[:, m * P:(m + 1) * P], acc[:, 0, m * P:(m + 1) * P], ident)
                elif kind == "pool":
                    m = name[1]
                    pe.wait_ge(pooled_ready, m // 2 + 1)
                    w = chunk(("pool",), 256)
                    for k in range(2):
                        for a, b in SEGS:
                            last = pe.matmul(bank[:, a:b], w[:, 2 * (m // 2) + k, (m % 2) * P:(m % 2 + 1) * P],
                                             sq[:, 2 * (m // 2) + k, a:b], start=k == 0, stop=k == 1)
                last.then_inc(full, 1)
                if kind == "wq" and name[2]:
                    scores(name[1], name[2] - 1)


def shape_constants():
    const = np.zeros((P, N_CONST), np.float32)
    const[:, C_ID:C_ID + P] = np.eye(P)
    const[:, C_ONE:C_ONE + P] = 1.0
    quarter = HD // 4
    for d in range(HD):
        axis, r = divmod(d, 2 * quarter)
        src = d + quarter if r < quarter else d - quarter
        const[src, C_ROT + d] = -1.0 if r < quarter else 1.0
    const[:, C_IO:C_IO + P] = np.arange(P)
    grid = 64
    f = np.power(np.float32(10000.0), -np.arange(quarter, dtype=np.float32) / np.float32(quarter)).astype(np.float32)
    t = np.arange(TS)
    ar = (t // grid).astype(np.float32)[None] * f[:, None]
    ac = (t % grid).astype(np.float32)[None] * f[:, None]
    ang = np.concatenate([ar, ar, ac, ac])
    trig = np.stack([np.cos(ang), np.sin(ang)], 1).astype(np.float32)
    inv = np.zeros((4, T), np.float32)
    for j, w in enumerate(WINDOWS):
        for a, b in SEGS:
            s = b - a
            q = np.arange(s)
            inv[j, a:b] = 1.0 / (np.clip(q + w // 2, 0, s) - np.clip(q - w // 2, 0, s))
    return const, trig, np.broadcast_to(inv, (P, 4, T)).copy()


def kernel(x_prompt, x_sample, cache_k, cache_v, c, c_ctx, ada_w, ada_b, norm_mix_g, norm_ffn_g,
           final_norm_g, attn_w_qkv, attn_q_norm_g, attn_k_norm_g, attn_w_o, pool_w, pool_scale,
           peer_wq, peer_keys, peer_u, peer_v):
    import concourse.bacc as _bacc
    from concourse.bass_utils import run_bass_kernel_spmd as _run

    arr = {k: np.asarray(v) for k, v in locals().items() if not k.startswith("_")}
    cols = lambda a: np.ascontiguousarray(a.reshape(-1, P).T)
    rows = lambda w, n: np.ascontiguousarray(
        w.reshape(K, P, w.shape[-1] // n, n).transpose(2, 1, 0, 3)).reshape(w.shape[-1] // n, P, K * n)
    x = np.concatenate([arr["x_sample"][0], arr["x_prompt"][0]])
    xT = np.ascontiguousarray(x.T.reshape(K, P, T).transpose(1, 0, 2))
    cond = np.stack([cols(arr["c"][0]), cols(arr["c_ctx"])], 2).reshape(P, 2 * K)
    gains = [arr["norm_mix_g"][0], arr["norm_ffn_g"][0], arr["norm_mix_g"][1], arr["norm_ffn_g"][1], arr["final_norm_g"]]
    small = np.concatenate(
        [cond, cols(arr["ada_b"])] + [cols(g) for g in gains]
        + [arr["attn_q_norm_g"].T, arr["attn_k_norm_g"].T, cols(arr["pool_scale"])], 1)
    const, trig, inv = shape_constants()
    ck = np.ascontiguousarray(arr["cache_k"][0, 0].transpose(2, 1, 0))
    cv = np.ascontiguousarray(arr["cache_v"][0, 0]).reshape(P, NKV * HD)
    ada = np.stack([rows(w, CH) for w in arr["ada_w"]])
    qkv = rows(arr["attn_w_qkv"][0], CH)
    wo = rows(arr["attn_w_o"][0], CH)
    pw = np.ascontiguousarray(arr["pool_w"][0].reshape(4, 2, P, 256).transpose(2, 0, 1, 3)).reshape(P, 2048)
    wq = np.stack([rows(w, CH) for w in arr["peer_wq"]])
    keys = np.ascontiguousarray(arr["peer_keys"].reshape(DEPTH, HP, NKEY, P).transpose(0, 3, 1, 2))
    uT = np.ascontiguousarray(arr["peer_u"].reshape(DEPTH, NKEY, P, K, P).transpose(0, 1, 4, 3, 2)
                              ).reshape(DEPTH, NKEY, P, D)
    ins = dict(xT=xT, small=small, const=const, trig=trig, inv=inv, ck=ck, cv=cv, ada=ada, qkv=qkv, wo=wo, pw=pw,
               wq=wq, keys=keys, u=arr["peer_u"], v=arr["peer_v"], uT=uT)
    outs = dict(yT=(P, K, T), nk=(P, NKV, P), nv=(P, NKV * HD))
    nc = _bacc.Bacc("TRN2", target_bir_lowering=False, num_devices=1)
    in_aps = [nc.dram_tensor("in_" + n, a.shape, F32, kind="ExternalInput").ap() for n, a in ins.items()]
    out_aps = [nc.dram_tensor("out_" + n, s, F32, kind="ExternalOutput").ap() for n, s in outs.items()]
    build(nc, in_aps, out_aps)
    r = _run(nc, [{"in_" + n: a for n, a in ins.items()}], core_ids=[0]).results[0]
    y = np.ascontiguousarray(np.asarray(r["out_yT"]).transpose(2, 1, 0)).reshape(T, D)
    new_k = np.asarray(r["out_nk"]).transpose(2, 1, 0).reshape(1, 1, TP, NKV, HD)
    new_v = np.asarray(r["out_nv"]).reshape(1, 1, TP, NKV, HD)
    return y[None, TS:], y[None, :TS], np.ascontiguousarray(new_k), new_v
```
